# Optimizing a Trainium2 kernel written in Bass

```python
import math
import jax, jax.numpy as jnp
from jax import lax
import numpy as np

D_MODEL = 1024
BATCH = 1
SEQ = 256
DEPTH = 2
DEC_BATCH = 1
DEC_SEQ = 256
PAST_LEN = 128

D_FF = 2816
CONF_WIDTH = D_MODEL
CONF_KERNEL = 31
SSD_EXPAND = 2
SSD_INNER = SSD_EXPAND * D_MODEL
SSD_HEAD_DIM = 64
SSD_HEADS = SSD_INNER // SSD_HEAD_DIM
SSD_GROUPS = 8
SSD_STATE = 128
SSD_CONV = 5
SSD_CHUNK = 128
SSD_CONV_DIM = SSD_INNER + 2 * SSD_GROUPS * SSD_STATE
N_IN = 2 * CONF_WIDTH + SSD_INNER + SSD_CONV_DIM + 2 * SSD_HEADS + 2 * D_MODEL
EPS = 1e-6

kernel_name = "hybrid_conformer_ssd_gated_encoder"

def _rms_norm(x, g):
    xf = x.astype(jnp.float32)
    y = xf * lax.rsqrt(jnp.mean(xf * xf, axis=-1, keepdims=True) + EPS)
    return (y * g.astype(jnp.float32)).astype(x.dtype)

def _layer_norm(x, g, b):
    xf = x.astype(jnp.float32)
    mu = jnp.mean(xf, axis=-1, keepdims=True)
    var = jnp.mean(jnp.square(xf - mu), axis=-1, keepdims=True)
    y = (xf - mu) * lax.rsqrt(var + EPS)
    return (y * g.astype(jnp.float32) + b.astype(jnp.float32)).astype(x.dtype)

def _gated_group_rms_norm(y, z, g):
    bsz, l, d = y.shape
    v = (y * jax.nn.silu(z)).astype(jnp.float32).reshape(bsz, l, SSD_GROUPS, d // SSD_GROUPS)
    v = v * lax.rsqrt(jnp.mean(v * v, axis=-1, keepdims=True) + EPS)
    return (v.reshape(bsz, l, d) * g.astype(jnp.float32)).astype(y.dtype)

def _swiglu(x, w_up, w_down):
    a, b = jnp.split(x @ w_up, 2, axis=-1)
    return (jax.nn.silu(a) * b) @ w_down

def _dwconv_centred(x, w, b):
    k = w.shape[0]
    y = lax.conv_general_dilated(
        x, w.astype(x.dtype)[:, None, :], window_strides=(1,),
        padding=[(k // 2, k // 2)], dimension_numbers=("NWC", "WIO", "NWC"),
        feature_group_count=x.shape[-1])
    return y + b.astype(x.dtype)

def _ssd_scan(x, dt, A, B, C):
    bsz, l, h, p = x.shape
    g, n = B.shape[-2:]
    r = h // g
    q = SSD_CHUNK
    c = l // q
    xc = x.reshape(bsz, c, q, g, r, p)
    dtc = dt.reshape(bsz, c, q, g, r)
    Bc = B.reshape(bsz, c, q, g, n)
    Cc = C.reshape(bsz, c, q, g, n)
    a = dtc * A.astype(jnp.float32).reshape(g, r)
    a_cum = jnp.cumsum(a, axis=2)
    xdt = xc.astype(jnp.float32) * dtc[..., None]
    seg = a_cum[:, :, :, None] - a_cum[:, :, None, :]
    tril = jnp.tril(jnp.ones((q, q), dtype=bool))[:, :, None, None]
    decay = jnp.exp(jnp.where(tril, seg, -jnp.inf))
    scores = jnp.einsum("bcign,bcjgn->bcijg", Cc, Bc).astype(jnp.float32)
    y_diag = jnp.einsum("bcijgr,bcjgrp->bcigrp", scores[..., None] * decay, xdt)
    decay_to_end = jnp.exp(a_cum[:, :, -1:] - a_cum)
    states = jnp.einsum("bcjgn,bcjgrp->bcgrpn", Bc.astype(jnp.float32),
                        xdt * decay_to_end[..., None])
    chunk_decay = jnp.exp(a_cum[:, :, -1])

    def step(s, inp):
        st, dec = inp
        return s * dec[..., None, None] + st, s

    s0 = jnp.zeros((bsz, g, r, p, n), jnp.float32)
    _, prev = lax.scan(step, s0, (jnp.moveaxis(states, 1, 0), jnp.moveaxis(chunk_decay, 1, 0)))
    prev = jnp.moveaxis(prev, 0, 1)
    y_off = jnp.einsum("bcign,bcgrpn->bcigrp", Cc.astype(jnp.float32), prev) * jnp.exp(a_cum)[..., None]
    return (y_diag + y_off).reshape(bsz, l, h, p).astype(x.dtype)

def _conformer_branch(p_glu, dw_w, dw_b, ln_g, ln_b, w_out):
    a, gate = jnp.split(p_glu, 2, axis=-1)
    v = a * jax.nn.sigmoid(gate)
    v = _dwconv_centred(v, dw_w, dw_b)
    v = jax.nn.silu(_layer_norm(v, ln_g, ln_b))
    return v @ w_out

def _ssd_branch(p_z, p_xbc, p_dt, conv_w, conv_b, dt_bias, A_log, D_skip, norm_g, w_out):
    bsz, l, _ = p_z.shape
    xbc = jax.nn.silu(_dwconv_centred(p_xbc, conv_w, conv_b))
    xs, Bm, Cm = jnp.split(xbc, [SSD_INNER, SSD_INNER + SSD_GROUPS * SSD_STATE], axis=-1)
    xs = xs.reshape(bsz, l, SSD_HEADS, SSD_HEAD_DIM)
    Bm = Bm.reshape(bsz, l, SSD_GROUPS, SSD_STATE)
    Cm = Cm.reshape(bsz, l, SSD_GROUPS, SSD_STATE)
    dt_raw = p_dt.astype(jnp.float32).reshape(bsz, l, 2, SSD_HEADS)
    dt = jax.nn.softplus(dt_raw + dt_bias.astype(jnp.float32))
    A = -jnp.exp(A_log.astype(jnp.float32))
    y_fwd = _ssd_scan(xs, dt[:, :, 0], A[0], Bm, Cm)
    flip = lambda t: jnp.flip(t, axis=1)
    y_bwd = flip(_ssd_scan(flip(xs), flip(dt[:, :, 1]), A[1], flip(Bm), flip(Cm)))
    y = y_fwd + y_bwd + xs * D_skip.astype(xs.dtype)[:, None]
    y = _gated_group_rms_norm(y.reshape(bsz, l, SSD_INNER), p_z, norm_g)
    return y @ w_out

def _trunk(x, ffn1_norm, ffn1_w_up, ffn1_w_down, mix_norm, w_in, gate_bias,
           conf_dw_w, conf_dw_b, conf_ln_g, conf_ln_b, conf_w_out,
           ssd_conv_w, ssd_conv_b, ssd_dt_bias, ssd_A_log, ssd_D, ssd_norm, ssd_w_out,
           w_o, ffn2_norm, ffn2_w_up, ffn2_w_down, final_norm):
    splits = [2 * CONF_WIDTH,
              2 * CONF_WIDTH + SSD_INNER,
              2 * CONF_WIDTH + SSD_INNER + SSD_CONV_DIM,
              2 * CONF_WIDTH + SSD_INNER + SSD_CONV_DIM + 2 * SSD_HEADS]
    for i in range(DEPTH):
        x = x + 0.5 * _swiglu(_rms_norm(x, ffn1_norm[i]), ffn1_w_up[i], ffn1_w_down[i])
        u = _rms_norm(x, mix_norm[i])
        proj = u @ w_in[i]
        p_glu, p_z, p_xbc, p_dt, p_gate = jnp.split(proj, splits, axis=-1)
        y_a = _conformer_branch(p_glu, conf_dw_w[i], conf_dw_b[i], conf_ln_g[i], conf_ln_b[i], conf_w_out[i])
        y_b = _ssd_branch(p_z, p_xbc, p_dt, ssd_conv_w[i], ssd_conv_b[i], ssd_dt_bias[i],
                          ssd_A_log[i], ssd_D[i], ssd_norm[i], ssd_w_out[i])
        g_a, g_b = jnp.split(jax.nn.sigmoid(p_gate + gate_bias[i]), 2, axis=-1)
        x = x + (g_a * y_a + g_b * y_b) @ w_o[i]
        x = x + 0.5 * _swiglu(_rms_norm(x, ffn2_norm[i]), ffn2_w_up[i], ffn2_w_down[i])
    return _rms_norm(x, final_norm)

def setup_inputs(seed: int = 0) -> dict:
    key = jax.random.key(seed)
    ks = jax.random.split(key, 32)
    f32 = jnp.float32
    nrm = lambda k, shape, s: jax.random.normal(k, shape, f32) * s
    gain = lambda k, shape: 1.0 + 0.02 * jax.random.normal(k, shape, f32)
    u_dt = jax.random.uniform(ks[20], (DEPTH, 2, SSD_HEADS), f32)
    dt0 = jnp.exp(u_dt * (math.log(0.1) - math.log(0.001)) + math.log(0.001))
    dt_bias = dt0 + jnp.log(-jnp.expm1(-dt0))
    A_log = jnp.log(jax.random.uniform(ks[21], (DEPTH, 2, SSD_HEADS), f32, minval=1.0, maxval=16.0))
    return {
        "x_prompt": jax.random.normal(ks[0], (BATCH, SEQ, D_MODEL), f32),
        "x_sample": jax.random.normal(ks[1], (DEC_BATCH, DEC_SEQ, D_MODEL), f32),
        "ffn1_norm": gain(ks[2], (DEPTH, D_MODEL)),
        "ffn1_w_up": nrm(ks[3], (DEPTH, D_MODEL, 2 * D_FF), D_MODEL ** -0.5),
        "ffn1_w_down": nrm(ks[4], (DEPTH, D_FF, D_MODEL), D_FF ** -0.5),
        "mix_norm": gain(ks[5], (DEPTH, D_MODEL)),
        "w_in": nrm(ks[6], (DEPTH, D_MODEL, N_IN), D_MODEL ** -0.5),
        "gate_bias": nrm(ks[7], (DEPTH, 2 * D_MODEL), 0.02),
        "conf_dw_w": nrm(ks[8], (DEPTH, CONF_KERNEL, CONF_WIDTH), CONF_KERNEL ** -0.5),
        "conf_dw_b": nrm(ks[9], (DEPTH, CONF_WIDTH), 0.02),
        "conf_ln_g": gain(ks[10], (DEPTH, CONF_WIDTH)),
        "conf_ln_b": nrm(ks[11], (DEPTH, CONF_WIDTH), 0.02),
        "conf_w_out": nrm(ks[12], (DEPTH, CONF_WIDTH, D_MODEL), CONF_WIDTH ** -0.5),
        "ssd_conv_w": nrm(ks[13], (DEPTH, SSD_CONV, SSD_CONV_DIM), SSD_CONV ** -0.5),
        "ssd_conv_b": nrm(ks[14], (DEPTH, SSD_CONV_DIM), 0.02),
        "ssd_dt_bias": dt_bias,
        "ssd_A_log": A_log,
        "ssd_D": 1.0 + 0.1 * jax.random.normal(ks[15], (DEPTH, SSD_HEADS), f32),
        "ssd_norm": gain(ks[16], (DEPTH, SSD_INNER)),
        "ssd_w_out": nrm(ks[17], (DEPTH, SSD_INNER, D_MODEL), SSD_INNER ** -0.5),
        "w_o": nrm(ks[18], (DEPTH, D_MODEL, D_MODEL), D_MODEL ** -0.5),
        "ffn2_norm": gain(ks[19], (DEPTH, D_MODEL)),
        "ffn2_w_up": nrm(ks[22], (DEPTH, D_MODEL, 2 * D_FF), D_MODEL ** -0.5),
        "ffn2_w_down": nrm(ks[23], (DEPTH, D_FF, D_MODEL), D_FF ** -0.5),
        "final_norm": gain(ks[24], (D_MODEL,)),
    }

def reference(x_prompt, x_sample, ffn1_norm, ffn1_w_up, ffn1_w_down, mix_norm, w_in, gate_bias,
              conf_dw_w, conf_dw_b, conf_ln_g, conf_ln_b, conf_w_out,
              ssd_conv_w, ssd_conv_b, ssd_dt_bias, ssd_A_log, ssd_D, ssd_norm, ssd_w_out,
              w_o, ffn2_norm, ffn2_w_up, ffn2_w_down, final_norm):
    params = (ffn1_norm, ffn1_w_up, ffn1_w_down, mix_norm, w_in, gate_bias,
              conf_dw_w, conf_dw_b, conf_ln_g, conf_ln_b, conf_w_out,
              ssd_conv_w, ssd_conv_b, ssd_dt_bias, ssd_A_log, ssd_D, ssd_norm, ssd_w_out,
              w_o, ffn2_norm, ffn2_w_up, ffn2_w_down, final_norm)
    y_prompt = _trunk(x_prompt, *params)
    y_sample = _trunk(x_sample, *params)
    return (y_prompt, y_sample)


_drawn_inputs = setup_inputs


def setup_inputs(seed=0):
    import zlib

    import numpy as np

    out = dict(_drawn_inputs(seed))
    spreads = {}
    factors = {'ffn1_norm': 4.079,
     'gate_bias': 8.0,
     'conf_dw_b': 3.501,
     'conf_ln_g': 27.127,
     'conf_ln_b': 28.727,
     'ssd_conv_b': 2.752,
     'ssd_norm': 19.461,
     'ffn2_norm': 5.839,
     'final_norm': 8.164}
    for name, (base, spread) in spreads.items():
        noise = np.random.default_rng([zlib.crc32(name.encode()), seed]).standard_normal(out[name].shape)
        drawn = base * np.exp(spread * noise) if base else spread * noise
        out[name] = __import__('jax').numpy.asarray(drawn.astype(out[name].dtype))
    for name, factor in factors.items():
        out[name] = (out[name] * factor).astype(out[name].dtype)
    return out
```

```python
from contextlib import ExitStack

import concourse.bass as bass
from concourse import mybir

F32 = mybir.dt.float32
F32R = mybir.dt.float32r
ALU = mybir.AluOpType
ACT = mybir.ActivationFunctionType

P = 128
RING = 4
AHEAD = 3
EPS = 1e-6
HEAD = 64
HPG = 4
TAPS = 5


def trunk(nc, io):
    x_prompt, x_sample = io["x_prompt"], io["x_sample"]
    SEQ, DM = x_prompt.shape[1:]
    DEPTH = io["w_in"].shape[0]
    FF = io["ffn1_w_down"].shape[1]
    DWK = io["conf_dw_w"].shape[1]
    HALO = DWK // 2
    T = 2 * SEQ
    KD = DM // P
    FT = FF // P
    NG = KD
    XT_ = 2 * KD
    NH = NG * HPG
    GF = HPG * HEAD
    NC = T // P
    CPR = SEQ // P
    assert T == 512 and CPR == 2 and DM == 1024 and DWK == 31
    C_A, C_GATE, C_Z = 0, DM, 2 * DM
    C_X = C_Z + 2 * DM
    C_B = C_X + 2 * DM
    C_C = C_B + DM
    C_DT = C_C + DM
    C_GA = C_DT + 2 * NH
    C_GB = C_GA + DM
    PARTS = [(0, 8), (8, 8), (16, FT - 16)]
    FFN_SLABS = 2 * FT + KD * len(PARTS)
    S_GROUP = FFN_SLABS
    S_SSDO = S_GROUP + 8 * NG
    S_GB = S_SSDO + 2 * KD
    S_GA = S_GB + KD
    S_CONF = S_GA + KD
    S_WO = S_CONF + KD
    S_FFN2 = S_WO + KD
    NSLAB = S_FFN2 + FFN_SLABS
    assert all(s % RING == 0 for s in (S_GROUP, S_SSDO, S_GB, S_GA, S_CONF, S_WO, S_FFN2, NSLAB))

    P_FFN1, P_MIX, P_FFN2, P_FIN = 0, KD, 2 * KD, 3 * KD
    P_LNG, P_LNB, P_DWB, P_SN = 4 * KD, 5 * KD, 6 * KD, 7 * KD
    P_CB = P_SN + XT_
    P_GBIAS = P_CB + 4 * KD
    P_DW = P_GBIAS + 2 * KD
    P_CW = P_DW + DWK * KD
    NPRM = P_CW + TAPS * 4 * KD

    BROWS = [P_DW, P, DWK * KD - P, P, TAPS * 4 * KD - P]
    PB = sum(BROWS[:-1])
    NCONST = DEPTH * 17 - 3
    ND = 11

    v_dram = nc.dram_tensor("v_spill", [2, KD, P, SEQ], F32, kind="Internal").ap()
    c_dram = nc.dram_tensor("conv_spill", [2, KD, P, SEQ], F32, kind="Internal").ap()
    y_dram = nc.dram_tensor("y_spill", [XT_, P, T], F32, kind="Internal").ap()

    kview = lambda w: w.rearrange("l (k p) f -> p (l k) f", p=P)
    W_UP = [kview(io["ffn1_w_up"]), kview(io["ffn2_w_up"])]
    W_DOWN = [kview(io["ffn1_w_down"]), kview(io["ffn2_w_down"])]
    W_IN, W_CONF, W_SSD, W_O = (kview(io[n]) for n in ("w_in", "conf_w_out", "ssd_w_out", "w_o"))

    with ExitStack() as ctx:
        def sb(name, shape, dt=F32, at=ctx):
            return at.enter_context(nc.sbuf_tensor(name, shape, dt))

        def sem(name):
            return ctx.enter_context(nc.semaphore(name))

        xf = sb("xf", [P, KD, T])
        wraw = sb("wraw", [P, RING, 8 * P])
        whi = sb("whi", [P, RING, 8 * P], F32R)
        wlo = sb("wlo", [P, RING, 8 * P], F32R)
        uhi = sb("uhi", [P, KD, T], F32R)
        ulo = sb("ulo", [P, KD, T], F32R)
        hhi = sb("hhi", [P, KD, T], F32R)
        hlo = sb("hlo", [P, KD, T], F32R)
        ident = sb("ident", [P, P])
        ones = sb("ones", [P, P])
        ul = sb("ul", [P, 2, P])
        selr = sb("selr", [P, 2, 2 * NH])
        rt = sb("rt", [P, NC, P], F32R)
        selg = sb("selg", [P, 2, 2, HPG], F32R)
        prm2 = sb("prm2", [P, DEPTH, NPRM])
        prm = sb("prm", [P, NPRM])
        rbc = sb("rbc", [P, T])
        sq = sb("sq", [P, 2, T])
        dtT = sb("dtT", [P, NC, 2 * NH])
        exT = sb("exT", [P, NC, 2 * NH])
        wT = sb("wT", [P, NC, 2 * NH])
        dtg = sb("dtg", [P, NC, 2, HPG])
        exg = sb("exg", [P, NC, HPG])
        wg = sb("wg", [P, NC, HPG])
        dskip = sb("dskip", [P, DEPTH * XT_])
        dtbA = sb("dtbA", [2 * NH, 2, DEPTH])
        negA = sb("negA", [2 * NH, DEPTH])
        hbias = sb("hbias", [P, 2 * KD])
        eps_t = sb("eps_t", [P, 1])
        vp = sb("vp", [P, SEQ + 2 * HALO])
        cacc = sb("cacc", [P, 2, SEQ])
        cwg = sb("cwg", [P, DWK])

        with ExitStack() as s0:
            stage = sb("stage", [P, DEPTH * 5, P], at=s0)
            x_tm = sb("x_tm", [P, NC, DM], at=s0)
            dall = sb("dall", [P, DEPTH, NH], at=s0)
        with ExitStack() as s1:
            fa = sb("fa", [P, 2, T], at=s1)
            fb = sb("fb", [P, 2, T], at=s1)
            s2 = s1
            wd_raw = sb("wd_raw", [P, 8, P], at=s2)
            wd_hi = sb("wd_hi", [P, 8, P], F32R, at=s2)
            wd_lo = sb("wd_lo", [P, 8, P], F32R, at=s2)
            dx = sb("dx", [2 * NH, T], at=s2)
            de = sb("de", [2 * NH, T], at=s2)
            du = sb("du", [2 * NH, T], at=s2)
            dl = sb("dl", [2 * NH, T], at=s2)
            dc = sb("dc", [2 * NH, T], at=s2)
            dtf = sb("dtf", [2 * NH, 2, T], at=s2)
            aT = sb("aT", [P, NC, 2 * NH], at=s2)
            cumS = sb("cumS", [P, NC, 2 * NH], at=s2)
            ddS = sb("ddS", [P, NC, 2 * NH], at=s2)
        with ExitStack() as s3:
            tg = sb("tg", [P, T], at=s3)
            xpad = sb("xpad", [P, 2, 2, SEQ + TAPS - 1], at=s3)
            bc = sb("bc", [P, 4, T], at=s3)
            yz = sb("yz", [P, 2, T], at=s3)
            znew = sb("znew", [P, 2, T], at=s3)
            zcur = sb("zcur", [P, 2, T], at=s3)
            xT = sb("xT", [P, NC, GF], at=s3)
            SUL = sb("SUL", [P, 2, NC, P], at=s3)
            st = sb("st", [P, NC, GF], at=s3)
            yoff = sb("yoff", [P, NC, GF], at=s3)
            ytm = sb("ytm", [P, 2, GF], at=s3)
            rg = sb("rg", [P, T], at=s3)
            with ExitStack() as s3a:
                E = sb("E", [P, 2, HPG, P], at=s3a)
                TM = sb("TM", [P, 2, HPG, P], at=s3a)
            with ExitStack() as s3b:
                xw = sb("xw", [P, NC, GF], at=s3b)
                bT = sb("bT", [P, NC, P], at=s3b)
        with ExitStack() as s4:
            mix = sb("mix", [P, KD, T], at=s4)
            with ExitStack() as s4y:
                yraw = sb("yraw", [P, 4, T], at=s4y)
            mtmp = sb("mtmp", [P, 2, T], at=s4)
            mu = sb("mu", [P, T], at=s4)
            rstd = sb("rstd", [P, T], at=s4)
            with ExitStack() as s4a:
                phi = sb("phi", [P, KD, T], F32R, at=s4a)
                plo = sb("plo", [P, KD, T], F32R, at=s4a)
            with ExitStack() as s4b:
                ga = sb("ga", [P, KD, T], at=s4b)
                cv = sb("cv", [P, KD, T], at=s4b)
        with ExitStack() as s5:
            yfin = sb("yfin", [P, KD, T], at=s5)
            o_tm = sb("o_tm", [P, NC, DM], at=s5)

        bank = [ctx.enter_context(nc.psum_tensor(f"bank{i}", [P, 512], F32)) for i in range(8)]

        pool_passed, pe_passed, dve_passed = (sem(n) for n in "pool_passed pe_passed dve_passed".split())
        raw_in = [sem(f"raw_in{i}") for i in range(RING)]
        yr_in = [sem(f"yr_in{i}") for i in range(4)]
        hi_ready, lo_ready, slab_done = (
            sem(n) for n in "hi_ready lo_ready slab_done".split())
        consts_in, const_made, const_fix, x_in, prm_ps, prm2_ready, negA_exp, negA_ready = (
            sem(n) for n in "consts_in const_made const_fix x_in prm_ps prm2_ready negA_exp negA_ready".split())
        prm_ready, x_ps, x_done = (
            sem(n) for n in "prm_ready x_ps x_done".split())
        sq_ready, stat_mm, lnr, r_ready, nt_ready, nhi_ready, u_ready = (
            sem(n) for n in "sq_ready stat_mm lnr r_ready nt_ready nhi_ready u_ready".split())
        ab_free, fa_ready, silu_ready, h_ready, hhi_ready, hlo_ready = (
            sem(n) for n in "ab_free fa_ready silu_ready h_ready hhi_ready hlo_ready".split())
        wd_in, wd_hi_ready, wd_lo_ready, dt_ps, dt_dve, dt_act, dtr_ps, dtr_ev, rt_ps, rt_hi = (
            sem(n) for n in "wd_in wd_hi_ready wd_lo_ready dt_ps dt_dve dt_act dtr_ps dtr_ev rt_ps rt_hi".split())
        rt_ready, cum_ps, ex_ready, wT_ready = (
            sem(n) for n in "rt_ready cum_ps ex_ready wT_ready".split())
        tg_ready, v_ready, v_out, pad_zero, pad_ready, cv_ready = (
            sem(n) for n in "tg_ready v_ready v_out pad_zero pad_ready cv_ready".split())
        conv_tap, bc_ready, z_ready, zcopied = (
            sem(n) for n in "conv_tap bc_ready z_ready zcopied".split())
        small_ready, xt_ps, bt_ps, sc_ps, xt_ready, bt_ready, sul_ready, xw_ready = (
            sem(n) for n in "small_ready xt_ps bt_ps sc_ps xt_ready bt_ready sul_ready xw_ready".split())
        st_ps, st_ready, yoff_ps, yoff_ready, seg_ps, seg_mid, seg_ready, e_ready = (
            sem(n) for n in "st_ps st_ready yoff_ps yoff_ready seg_ps seg_mid seg_ready e_ready".split())
        t1_ready, t2_ready, m_ready, y_ps, y_ready, yt_ps, gate_mid, gated, xd_ready = (
            sem(n) for n in "t1_ready t2_ready m_ready y_ps y_ready yt_ps gate_mid gated xd_ready".split())
        gsq, gst_ps, gln, gr_ready, y2_ready, y_out = (
            sem(n) for n in "gsq gst_ps gln gr_ready y2_ready y_out".split())
        vp_in, cw_ready, unit_tap, unit_done, c_out = (
            sem(n) for n in "vp_in cw_ready unit_tap unit_done c_out".split())
        yhi_ready, y_split, so_free, gt_free, mix_b = (
            sem(n) for n in "yhi_ready y_split so_free gt_free mix_b".split())
        cv_in, mu_ps, mu_ready, d_ready, lsq, lst_ps, lln, lr_ready, n_ready, ns_ready = (
            sem(n) for n in "cv_in mu_ps mu_ready d_ready lsq lst_ps lln lr_ready n_ready ns_ready".split())
        chi_ready, c_split, ya_mid, mix_ready, mhi_ready, m_split = (
            sem(n) for n in "chi_ready c_split ya_mid mix_ready mhi_ready m_split".split())
        fin_ready, out_ps, out_ready, out_done = (
            sem(n) for n in "fin_ready out_ps out_ready out_done".split())

        block = ctx.enter_context(nc.Block())
        UNITS = 2 * KD
        XL = 2 * KD * len(PARTS) + KD
        X_WO = KD * len(PARTS)
        TAP_SLICES = [(0, 6), (6, 12), (12, 17), (17, 22), (22, 27), (27, DWK)]
        f32 = lambda ap: ap.bitcast(F32)
        chunk = lambda c: slice(c * P, (c + 1) * P)

        @block.sync
        def _(sp):
            def load(s, slot, src):
                sp.wait_ge(lo_ready, s + 1)
                k = src.shape[1]
                dst = wraw[:, slot, 0:k * P].rearrange("p (k m) -> p k m", m=P)
                sp.dma_start(dst, src).then_inc(raw_in[slot], 16)

            for r in range(2):
                src = (x_prompt, x_sample)[r].rearrange("b (c p) d -> p (b c) d", p=P)
                sp.dma_start(x_tm[:, r * CPR:(r + 1) * CPR, :], src).then_inc(x_in, 16)

            def ffn(L, f, base):
                s = L * NSLAB + base
                for p0, n in PARTS:
                    with sp.Fori(0, n // 2) as i:
                        for q in range(4):
                            col = i * (2 * P) + ((p0 + q // 2) * P + (q % 2) * FF)
                            load(s + i * 4 + q, q, W_UP[f][:, bass.ds(L * KD, KD), bass.ds(col, P)])
                    s = s + 2 * n
                    with sp.Fori(0, KD // 4) as i:
                        for q in range(4):
                            load(s + i * 4 + q, q,
                                 W_DOWN[f][:, bass.ds(L * FT + p0, n), bass.ds(i * (4 * P) + q * P, P)])
                    s = s + KD

            def columns(L, base, w, col):
                with sp.Fori(0, KD // 4) as i:
                    for q in range(4):
                        load(L * NSLAB + base + i * 4 + q, q,
                             w[:, bass.ds(L * KD, 8), bass.ds(i * (4 * P) + (q * P + col), P)])

            with sp.Fori(0, DEPTH) as L:
                ffn(L, 0, 0)
                with sp.Fori(0, NG) as g:
                    s = L * NSLAB + g * 8 + S_GROUP
                    cols = [g * P + C_GATE, g * P + C_A, g * (2 * P) + C_Z, g * (2 * P) + (C_Z + P),
                            g * P + C_B, g * P + C_C, g * (2 * P) + C_X, g * (2 * P) + (C_X + P)]
                    for t in range(8):
                        load(s + t, t % RING, W_IN[:, bass.ds(L * KD, 8), bass.ds(cols[t], P)])
                with sp.Fori(0, KD // 2) as i:
                    for q in range(4):
                        load(L * NSLAB + S_SSDO + i * 4 + q, q,
                             W_SSD[:, bass.ds(L * XT_ + 8 * (q % 2), 8), bass.ds(i * (2 * P) + (q // 2) * P, P)])
                columns(L, S_GB, W_IN, C_GB)
                columns(L, S_GA, W_IN, C_GA)
                columns(L, S_CONF, W_CONF, 0)
                columns(L, S_WO, W_O, 0)
                ffn(L, 1, S_FFN2)
            for q in range(AHEAD):
                load(DEPTH * NSLAB + q, q, W_UP[0][:, 0:KD, q * P:(q + 1) * P])
            for c in range(NC):
                sp.wait_ge(out_ready, 2 * (c + 1))
                dst = io["out_0"] if c < CPR else io["out_1"]
                sp.dma_start(dst[0, (c % CPR) * P:(c % CPR + 1) * P, :], o_tm[:, c, :]).then_inc(out_done, 16)
            sp.wait_ge(out_done, 16 * NC)

        @block.gpsimd
        def _(pool):
            g_ = nc.gpsimd
            for free, n in ((lo_ready, RING), (slab_done, RING), (stat_mm, 2), (ab_free, 2), (pad_ready, 2), (cv_ready, 2),
                            (conv_tap, 1), (zcopied, 1), (xt_ps, 1), (xw_ready, 1), (yoff_ps, 1), (yoff_ready, 1),
                            (seg_ps, 1), (seg_ready, 1), (m_ready, 1), (y_ps, 2), (y_ready, 1), (yt_ps, 2), (gated, 1),
                            (gst_ps, 1), (y2_ready, 1), (unit_tap, 1), (unit_done, 1), (y_split, 4), (so_free, 2),
                            (gt_free, 2), (mix_b, 2), (lst_ps, 2), (ya_mid, 2)):
                pool.sem_inc(free, n)
            g_.memset(ident[:, :], 0.0).then_inc(const_made, 1)
            g_.memset(ones[:, :], 1.0).then_inc(const_made, 1)
            g_.memset(ul[:, :, :], 1.0).then_inc(const_made, 1)
            g_.memset(selr[:, :, :], 0.0).then_inc(const_made, 1)
            g_.memset(eps_t[:, :], EPS).then_inc(const_made, 1)
            g_.memset(vp[:, :], 0.0).then_inc(const_made, 1)
            pool.wait_ge(const_made, 6)
            g_.affine_select(out=ident[:, :], in_=ident[:, :], compare_op=ALU.not_equal, fill=1.0, base=0,
                             pattern=[[-1, P]], channel_multiplier=1).then_inc(const_fix, 1)
            g_.affine_select(out=ul[:, 0, :], in_=ul[:, 0, :], compare_op=ALU.is_ge, fill=0.0, base=0,
                             pattern=[[1, P]], channel_multiplier=-1).then_inc(const_fix, 1)
            g_.affine_select(out=ul[:, 1, :], in_=ul[:, 1, :], compare_op=ALU.is_ge, fill=0.0, base=0,
                             pattern=[[-1, P]], channel_multiplier=1).then_inc(const_fix, 1)
            n = 3
            for sign in range(2):
                for half in range(2):
                    pool.wait_ge(const_fix, n)
                    pool.sem_inc(pool_passed, 1)
                    g_.affine_select(out=selr[:, sign, :], in_=selr[:, sign, :], compare_op=ALU.not_equal,
                                     fill=1.0 - 2 * sign, base=-half * 2 * NH, pattern=[[-1, 2 * NH]],
                                     channel_multiplier=1).then_inc(const_fix, 1)
                    n += 1
            names = ["ffn1_norm", "mix_norm", "ffn2_norm", None, "conf_ln_g", "conf_ln_b", "conf_dw_b",
                     "ssd_norm", "ssd_conv_b", "gate_bias"]
            credits = {(0, "ffn1_norm"): v_out, (0, "mix_norm"): y_out, (0, "ffn2_norm"): c_out}
            for l in range(DEPTH):
                row = 0
                for name in names:
                    src = (io["final_norm"] if name is None else io[name][l]).rearrange("(t p) -> t p", p=P)
                    n = src.shape[0]
                    g_.dma_start(stage[row:row + n, 5 * l, :], src).then_inc(credits.get((l, name), consts_in), 16)
                    row += n
                for b, name in ((1, "conf_dw_w"), (3, "ssd_conv_w")):
                    src = io[name][l].rearrange("k (t p) -> (k t) p", p=P)
                    g_.dma_start(stage[0:P, 5 * l + b, :], src[0:P]).then_inc(consts_in, 16)
                    g_.dma_start(stage[0:src.shape[0] - P, 5 * l + b + 1, :], src[P:]).then_inc(consts_in, 16)
                g_.dma_start(dall[:, l, :], io["ssd_D"][l:l + 1, :].broadcast_to([P, NH])).then_inc(consts_in, 16)
                for j, name in enumerate(("ssd_dt_bias", "ssd_A_log")):
                    g_.dma_start(dtbA[:, j, l:l + 1],
                                 io[name][l].rearrange("d (h o) -> (d h) o", o=1)).then_inc(consts_in, 16)

            def unit_load(L, U, r, tile):
                pool.wait_ge(unit_done, U + 1)
                pool.sem_inc(pool_passed, 1)
                pool.dma_start(vp[:, HALO:HALO + SEQ],
                               v_dram[r, bass.ds(tile, 1)].rearrange("o p t -> p (o t)")).then_inc(vp_in, 16)

            def unit_store(L, U, r, tile):
                pool.wait_ge(unit_done, U + 2)
                pool.sem_inc(pool_passed, 1)
                pool.dma_start(c_dram[r, bass.ds(tile, 1)].rearrange("o p t -> p (o t)"),
                               cacc[:, 0, :]).then_inc(c_out, 16)

            def group(L, g, slabs, ssd, norm):
                G = L * NG + g
                H = G - 1
                if ssd:
                    pool.wait_ge(m_ready, H * NC + 1)
                    pool.wait_ge(seg_ps, H * NC + 1)
                    pool.wait_ge(yoff_ready, H * 2 + 1)
                    pool.wait_ge(xw_ready, H + 1)
                    pool.wait_ge(dtr_ev, L * 2 + 2)
                    pool.wait_ge(ex_ready, L + 1)
                    pool.wait_ge(wT_ready, L + 1)
                    pool.sem_inc(pool_passed, 1)
                    h0 = g * HPG - HPG
                    src = dtT[:, :, :].rearrange("p c (d h) -> p c d h", d=2)[:, :, :, bass.ds(h0, HPG)]
                    g_.tensor_copy(dtg[:, :, :, :], src).then_inc(small_ready, 1)
                    src = exT[:, :, :].rearrange("p (b c) x -> p b (c x)", b=2)[:, :, NH:3 * NH]
                    src = src.rearrange("p b (c h) -> p b c h", c=2)[:, :, :, bass.ds(h0, HPG)]
                    g_.tensor_copy(exg[:, :, :].rearrange("p (b c) h -> p b c h", b=2), src).then_inc(small_ready, 1)
                    for c in range(2):
                        src = wT[:, c:NC:2, bass.ds(h0 + c * NH, HPG)]
                        g_.tensor_copy(wg[:, c:NC:2, :], src).then_inc(small_ready, 1)
                    src = selr[:, :, :].rearrange("p s (d h) -> p s d h", d=2)[:, :, :, bass.ds(h0, HPG)]
                    g_.tensor_copy(selg[:, :, :, :], src).then_inc(small_ready, 1)
                    pool.wait_ge(v_out, G * 16 + 16)
                    pool.sem_inc(pool_passed, 1)
                    unit_load(L, L * UNITS + g - 1, 0, g - 1)
                    pool.wait_ge(z_ready, H * 2 + 2)
                    pool.wait_ge(gated, H * NC + 1)
                    pool.sem_inc(pool_passed, 1)
                    for j in range(2):
                        g_.tensor_copy(zcur[:, j, :], znew[:, j, :]).then_inc(zcopied, 1)
                if slabs:
                    pool.wait_ge(v_ready, G + 1)
                    pool.sem_inc(pool_passed, 1)
                    pool.dma_start(v_dram[:, bass.ds(g, 1)].rearrange("r o p t -> p (r o) t"),
                                   tg[:, :].rearrange("p (r t) -> p r t", r=2)).then_inc(v_out, 16)
                if norm:
                    pool.wait_ge(y2_ready, G * 2 - 1)
                    pool.sem_inc(pool_passed, 1)
                    pool.dma_start(y_dram[bass.ds(g * 2 - 4, 2)].rearrange("k p t -> p k t"),
                                   yz[:, :, :]).then_inc(y_out, 16)
                if ssd:
                    pool.wait_ge(sul_ready, H * 2 + 2)
                    pool.wait_ge(st_ps, H * 2 + 2)
                    pool.sem_inc(pool_passed, 1)
                    for c in range(NC):
                        pool.wait_ge(y_ps, H * NC + c + 1)
                        pool.sem_inc(pool_passed, 1)
                        for h in range(HPG):
                            g_.tensor_scalar(TM[:, c % 2, h, :], SUL[:, 1, c, :], dtg[:, c, 1, h:h + 1], 1.0,
                                             ALU.mult, ALU.mult).then_inc(t1_ready, 1)
                    unit_store(L, L * UNITS + g - 1, 0, g - 1)

            with pool.Fori(0, DEPTH) as L:
                pool.wait_ge(x_done, L * XL + KD)
                pool.sem_inc(pool_passed, 1)
                pool.dma_start(wd_raw[:, :, :], W_IN[:, bass.ds(L * KD, KD), C_DT:C_DT + P]).then_inc(wd_in, 16)
                group(L, 0, True, False, False)
                group(L, 1, True, True, False)
                with pool.Fori(2, NG) as g:
                    group(L, g, True, True, True)
                group(L, NG, False, True, True)
                group(L, NG + 1, False, False, True)
                pool.wait_ge(y_out, (L * NG + NG) * 16 + 16)
                pool.sem_inc(pool_passed, 1)
                with pool.Fori(0, XT_ // 4) as i:
                    for q in range(4):
                        Y = L * XT_ + i * 4 + q
                        pool.wait_ge(y_split, Y + 1)
                        pool.sem_inc(pool_passed, 1)
                        pool.dma_start(yraw[:, q, :], y_dram[bass.ds(i * 4 + q, 1)].rearrange("o p t -> p (o t)")).then_inc(yr_in[q], 16)
                with pool.Fori(0, KD) as j:
                    unit_load(L, L * UNITS + KD + j, 1, j)
                    unit_store(L, L * UNITS + KD + j, 1, j)
                pool.wait_ge(c_out, (L * UNITS + UNITS) * 16 + 16)
                pool.wait_ge(slab_done, L * NSLAB + S_GB + RING)
                pool.sem_inc(pool_passed, 1)
                for r in range(2):
                    pool.dma_start(cv[:, :, r * SEQ:(r + 1) * SEQ],
                                   c_dram[r].rearrange("k p t -> p k t")).then_inc(cv_in, 16)

        @block.scalar
        def _(act):
            a_ = nc.scalar

            def split(s4, q):
                t = q + AHEAD
                act.wait_ge(raw_in[t % RING], s4 * 16 + 16 * (t // RING + 1))
                act.wait_ge(slab_done, s4 * 4 + (t + 1))
                a_.activation(whi[:, t % RING, :], wraw[:, t % RING, :], ACT.Copy).then_inc(hi_ready, 1)

            act.wait_ge(const_made, 6)
            for t in range(AHEAD):
                act.wait_ge(raw_in[t], 16)
                a_.activation(whi[:, t, :], wraw[:, t, :], ACT.Copy).then_inc(hi_ready, 1)
            for l in range(DEPTH):
                act.wait_ge(prm_ps, 2 * l + 1)
                a_.activation(prm2[:, l, 0:PB], bank[2 + 2 * l][:, 0:PB], ACT.Copy).then_inc(prm2_ready, 1)
                act.wait_ge(prm_ps, 2 * l + 2)
                a_.activation(prm2[:, l, PB:NPRM], bank[3 + 2 * l][:, 0:NPRM - PB], ACT.Copy).then_inc(prm2_ready, 1)
            for half in range(2):
                rows = slice(half * HEAD, (half + 1) * HEAD)
                a_.activation(dskip[rows, :].rearrange("p (l t) -> p l t", l=DEPTH), dall[rows, :, half:NH:2], ACT.Copy).then_inc(prm2_ready, 1)
            a_.activation(negA[:, :], dtbA[:, 1, :], ACT.Exp).then_inc(negA_exp, 1)

            def norm_squares(N, x_base):
                for k in range(KD):
                    act.wait_ge(x_done, x_base + k + 1)
                    act.wait_ge(stat_mm, N * KD + k + 1)
                    a_.activation(sq[:, k % 2, :], xf[:, k, :], ACT.Square).then_inc(sq_ready, 1)

            def norm_root(N):
                act.wait_ge(stat_mm, N * KD + KD + 2)
                a_.activation(rbc[:, :], bank[6][:, :], ACT.Ln, scale=1.0 / DM, bias=eps_t[:, 0:1]).then_inc(lnr, 1)
                act.wait_ge(lnr, N + 1)
                a_.activation(rbc[:, :], rbc[:, :], ACT.Exp, scale=-0.5).then_inc(r_ready, 1)

            def ffn(L, f, base):
                N = L * 3 + 2 * f
                xb = L * XL + (KD - KD if f == 0 else X_WO + KD)
                g0 = P_FFN1 if f == 0 else P_FFN2
                act.wait_ge(prm_ready, L * 2 + 2)
                for k in range(KD):
                    act.wait_ge(x_done, xb + k + 1)
                    act.wait_ge(stat_mm, N * KD + k + 1)
                    a_.activation(sq[:, k % 2, :], xf[:, k, :], ACT.Square).then_inc(sq_ready, 1)
                    if k == 0:
                        act.wait_ge(slab_done, L * NSLAB + base + RING)
                    a_.activation(uhi[:, k, :], xf[:, k, :], ACT.Copy, scale=prm[:, g0 + k:g0 + k + 1]).then_inc(nhi_ready, 1)
                norm_root(N)
                s4 = L * (NSLAB // 4) + base // 4
                for part, (p0, n) in enumerate(PARTS):
                    with act.Fori(0, n // 2) as i:
                        for j in range(2):
                            PI = L * (2 * FT) + (f * FT + p0 + j) + i * 2
                            split(s4 + i, 2 * j)
                            act.wait_ge(fa_ready, PI + 1)
                            a_.activation(fa[:, j, :], fa[:, j, :], ACT.Silu).then_inc(silu_ready, 1)
                            split(s4 + i, 2 * j + 1)
                            act.wait_ge(h_ready, PI + 1)
                            a_.activation(hhi[:, bass.ds(i * 2 + j, 1), :], fb[:, j:j + 1, :], ACT.Copy).then_inc(hhi_ready, 1)
                    s4 = s4 + n // 2
                    with act.Fori(0, KD // 4) as i:
                        for q in range(4):
                            split(s4 + i, q)
                    s4 = s4 + KD // 4

            def group(L, g, slabs, ssd, norm):
                G = L * NG + g
                H, n = G - 1, G - 2
                s4 = L * (NSLAB // 4) + g * 2 + S_GROUP // 4

                def step(t):
                    split(s4 + t // 4, t % 4)
                    act.wait_ge(slab_done, (s4 + t // 4) * 4 + (t % 4 + 1) + RING)

                def conv_silu(GG, j):
                    act.wait_ge(cv_ready, GG * 4 + j + 3)
                    a_.activation(bc[:, j, :], bc[:, j, :], ACT.Silu).then_inc(bc_ready, 1)

                def exp_seg(c):
                    act.wait_ge(seg_ready, H * NC + c + 2)
                    a_.activation(E[:, c % 2], E[:, c % 2], ACT.Exp).then_inc(e_ready, 1)

                if norm:
                    act.wait_ge(gated, n * NC + NC + 1)
                    act.wait_ge(gst_ps, n + 1)
                    for j in range(2):
                        a_.activation(sq[:, j, :], yz[:, j, :], ACT.Square).then_inc(gsq, 1)
                if ssd:
                    conv_silu(H, 3)
                if slabs:
                    step(0)
                    act.wait_ge(v_out, G * 16 + 16)
                    a_.activation(tg[:, :], bank[0][:, :], ACT.Tanh, scale=0.5).then_inc(tg_ready, 1)
                if ssd:
                    for b in range(2):
                        act.wait_ge(xt_ps, H * 2 + b + 2)
                        a_.activation(xT[:, 2 * b:2 * b + 2, :], bank[2 + b][:, :].rearrange("p (c f) -> p c f", c=2),
                                      ACT.Copy).then_inc(xt_ready, 1)
                    act.wait_ge(bt_ps, H + 1)
                    a_.activation(bT[:, :, :], bank[4][:, :].rearrange("p (c f) -> p c f", c=NC), ACT.Copy).then_inc(bt_ready, 1)
                if slabs:
                    split(s4, 1)
                if norm:
                    act.wait_ge(gst_ps, n + 2)
                    act.wait_ge(y2_ready, n * 2 + 1)
                    a_.activation(rg[:, :], bank[4][:, :], ACT.Ln, scale=1.0 / GF, bias=eps_t[:, 0:1]).then_inc(gln, 1)
                    act.wait_ge(gln, n + 1)
                    a_.activation(rg[:, :], rg[:, :], ACT.Exp, scale=-0.5).then_inc(gr_ready, 1)
                if ssd:
                    for b in range(2):
                        act.wait_ge(st_ps, H * 2 + b + 1)
                        a_.activation(st[:, 2 * b:2 * b + 2, :], bank[6 + b][:, :].rearrange("p (c f) -> p c f", c=2),
                                      ACT.Copy).then_inc(st_ready, 1)
                if slabs:
                    for t in (2, 3):
                        step(t)
                        if t == 2:
                            act.wait_ge(zcopied, G * 2 + 1)
                        a_.activation(znew[:, t - 2, :], bank[t % 2][:, :], ACT.Silu).then_inc(z_ready, 1)
                        if t == 2 and ssd:
                            exp_seg(0)
                        if t == 3 and ssd:
                            exp_seg(1)
                elif ssd:
                    exp_seg(0)
                    exp_seg(1)
                for t in range(4, 8):
                    if slabs:
                        step(t)
                        act.wait_ge(pad_zero, L + 1)
                        act.wait_ge(cv_ready, G * 4 + t - 3)
                        a_.activation(xpad[:, t % 2, :, 2:2 + SEQ], bank[t % 2][:, :].rearrange("p (r t) -> p r t", r=2),
                                      ACT.Copy).then_inc(pad_ready, 1)
                        if t > 4:
                            conv_silu(G, t - 5)
                    if ssd and t < 6:
                        exp_seg(t - 2)

            with act.Fori(0, DEPTH) as L:
                ffn(L, 0, 0)
                act.wait_ge(wd_in, L * 16 + 16)
                a_.activation(wd_hi[:, :, :], wd_raw[:, :, :], ACT.Copy).then_inc(wd_hi_ready, 1)
                N = L * 3 + 1
                norm_squares(N, L * XL + X_WO)
                norm_root(N)
                for k in range(KD):
                    act.wait_ge(nt_ready, L * KD + k + 1)
                    a_.activation(uhi[:, k, :], sq[:, k % 2, :], ACT.Copy).then_inc(nhi_ready, 1)
                act.wait_ge(dt_dve, L * ND + 1)
                a_.activation(de[:, :], dx[:, :], ACT.Abs).then_inc(dt_act, 1)
                act.wait_ge(dt_act, L * 5 + 1)
                a_.activation(de[:, :], de[:, :], ACT.Exp, scale=-1.0).then_inc(dt_act, 1)
                act.wait_ge(dt_dve, L * ND + 2)
                a_.activation(dl[:, :], du[:, :], ACT.Ln).then_inc(dt_act, 1)
                act.wait_ge(dtr_ps, L + 1)
                a_.activation(dtT[:, :, :], bank[1][:, 0:2 * T // 4].rearrange("p (c x) -> p c x", c=NC), ACT.Copy).then_inc(dtr_ev, 1)
                a_.activation(aT[:, :, :], bank[1][:, 2 * T // 4:].rearrange("p (c x) -> p c x", c=NC), ACT.Copy).then_inc(dtr_ev, 1)
                act.wait_ge(rt_ps, L + 1)
                for b in range(2):
                    for d in range(2):
                        rows = slice(d * NH, (d + 1) * NH)
                        src = bank[2 + b][rows, :].rearrange("p (c d i) -> p c d i", c=2, d=2)[:, :, d, :]
                        a_.activation(rt[rows, 2 * b:2 * b + 2, :], src, ACT.Copy).then_inc(rt_hi, 1)
                act.wait_ge(cum_ps, L + 1)
                a_.activation(cumS[:, :, :], bank[4][:, 0:256].rearrange("p (c x) -> p c x", c=NC), ACT.Copy).then_inc(dt_act, 1)
                act.wait_ge(dt_act, L * 5 + 4)
                a_.activation(exT[:, :, :], cumS[:, :, :], ACT.Exp).then_inc(ex_ready, 1)
                act.wait_ge(dt_dve, L * ND + 11)
                a_.activation(ddS[:, :, :], ddS[:, :, :], ACT.Exp).then_inc(dt_act, 1)
                group(L, 0, True, False, False)
                group(L, 1, True, True, False)
                with act.Fori(2, NG) as g:
                    group(L, g, True, True, True)
                group(L, NG, False, True, True)
                group(L, NG + 1, False, False, True)
                for k in range(XT_):
                    act.wait_ge(yr_in[k % 4], L * (XT_ // 4 * 16) + 16 * (k // 4 + 1))
                    dst = hhi[:, k, :] if k < KD else phi[:, k - KD, :]
                    a_.activation(dst, yraw[:, k % 4, :], ACT.Copy).then_inc(yhi_ready, 1)
                s4 = L * (NSLAB // 4)
                with act.Fori(0, KD // 2) as i:
                    for q in range(4):
                        split(s4 + S_SSDO // 4 + i, q)
                        if q % 2:
                            act.wait_ge(slab_done, (s4 + i) * 4 + (S_SSDO + q + 1) + RING)
                            a_.activation(mix[:, bass.ds(i * 2 + q // 2, 1), :], bank[2 + q // 2][:, :].unsqueeze(1), ACT.Copy).then_inc(so_free, 1)
                with act.Fori(0, KD // 4) as i:
                    for q in range(4):
                        split(s4 + S_GB // 4 + i, q)
                        act.wait_ge(slab_done, (s4 + i) * 4 + (S_GB + q + 1) + RING)
                        act.wait_ge(mix_b, L * KD + i * 4 + q + 1)
                        a_.activation(mtmp[:, q % 2, :], bank[4 + q % 2][:, :], ACT.Tanh, scale=0.5,
                                      bias=hbias[:, bass.ds(i * 4 + (KD + q), 1)]).then_inc(gt_free, 1)
                with act.Fori(0, KD // 4) as i:
                    for q in range(4):
                        split(s4 + S_GA // 4 + i, q)
                        act.wait_ge(slab_done, (s4 + i) * 4 + (S_GA + q + 1) + RING)
                        a_.activation(ga[:, bass.ds(i * 4 + q, 1), :], bank[4 + q % 2][:, :].unsqueeze(1), ACT.Tanh, scale=0.5,
                                      bias=hbias[:, bass.ds(i * 4 + q, 1)]).then_inc(gt_free, 1)
                act.wait_ge(mu_ps, L + 1)
                a_.activation(mu[:, :], bank[6][:, :], ACT.Copy, scale=1.0 / DM).then_inc(mu_ready, 1)
                for k in range(KD):
                    act.wait_ge(d_ready, L * KD + k + 1)
                    act.wait_ge(lst_ps, L * KD + k + 1)
                    a_.activation(sq[:, k % 2, :], cv[:, k, :], ACT.Square).then_inc(lsq, 1)
                act.wait_ge(lst_ps, L * KD + KD + 2)
                a_.activation(rstd[:, :], bank[7][:, :], ACT.Ln, scale=1.0 / DM, bias=eps_t[:, 0:1]).then_inc(lln, 1)
                act.wait_ge(lln, L + 1)
                a_.activation(rstd[:, :], rstd[:, :], ACT.Exp, scale=-0.5).then_inc(lr_ready, 1)
                for k in range(KD + 1):
                    if k < KD:
                        act.wait_ge(n_ready, L * KD + k + 1)
                        a_.activation(cv[:, k, :], cv[:, k, :], ACT.Silu, scale=prm[:, P_LNG + k:P_LNG + k + 1],
                                      bias=prm[:, P_LNB + k:P_LNB + k + 1]).then_inc(ns_ready, 1)
                    if k:
                        act.wait_ge(ns_ready, L * KD + k)
                        a_.activation(hhi[:, k - 1, :], cv[:, k - 1, :], ACT.Copy).then_inc(chi_ready, 1)
                with act.Fori(0, KD // 4) as i:
                    for q in range(4):
                        split(s4 + S_CONF // 4 + i, q)
                        act.wait_ge(mix_ready, L * KD + i * 4 + q + 1)
                        m = bass.ds(i * 4 + q, 1)
                        a_.activation(uhi[:, m, :], mix[:, m, :], ACT.Copy).then_inc(mhi_ready, 1)
                with act.Fori(0, KD // 4) as i:
                    for q in range(4):
                        split(s4 + S_WO // 4 + i, q)
                ffn(L, 1, S_FFN2)
            norm_squares(3 * DEPTH, DEPTH * XL)
            norm_root(3 * DEPTH)
            for c in range(NC):
                for half in range(2):
                    b = (2 * c + half) % 4
                    act.wait_ge(out_ps, 2 * c + half + 1)
                    a_.activation(o_tm[:, c, half * 512:(half + 1) * 512], bank[b][:, :], ACT.Copy).then_inc(out_ready, 1)

        @block.vector
        def _(dve):
            v_ = nc.vector

            def split(s4, q):
                t = q + AHEAD
                dve.wait_ge(hi_ready, s4 * 4 + (t + 1))
                v_.tensor_tensor(wlo[:, t % RING, :], wraw[:, t % RING, :], f32(whi[:, t % RING, :]), ALU.subtract).then_inc(lo_ready, 1)

            for t in range(AHEAD):
                dve.wait_ge(hi_ready, t + 1)
                v_.tensor_tensor(wlo[:, t, :], wraw[:, t, :], f32(whi[:, t, :]), ALU.subtract).then_inc(lo_ready, 1)
            for m in range(KD):
                dve.wait_ge(x_ps, m + 1)
                v_.tensor_copy(xf[:, m, :], bank[m % 2][:, :]).then_inc(x_done, 1)
            dve.wait_ge(negA_exp, 1)
            v_.tensor_scalar(negA[:, :], negA[:, :], -1.0, None, ALU.mult).then_inc(negA_ready, 1)
            dve.wait_ge(negA_ready, 1)

            def norm_low(N, g0):
                for k in range(KD):
                    dve.wait_ge(nhi_ready, N * KD + k + 1)
                    v_.scalar_tensor_tensor(out=ulo[:, k, :], in0=xf[:, k, :], scalar=prm[:, g0 + k:g0 + k + 1],
                                            in1=f32(uhi[:, k, :]), op0=ALU.mult, op1=ALU.subtract).then_inc(u_ready, 1)

            def ffn(L, f, base):
                N = L * 3 + 2 * f
                xb = L * XL + (KD if f == 0 else X_WO + 2 * KD)
                norm_low(N, P_FFN1 if f == 0 else P_FFN2)
                dve.wait_ge(r_ready, N + 1)
                dve.sem_inc(dve_passed, 1)
                s4 = L * (NSLAB // 4) + base // 4
                for part, (p0, n) in enumerate(PARTS):
                    with dve.Fori(0, n // 2) as i:
                        for j in range(2):
                            PI = L * (2 * FT) + (f * FT + p0 + j) + i * 2
                            split(s4 + i, 2 * j)
                            dve.wait_ge(slab_done, (s4 + i) * 4 + 2 * j + 1 + RING)
                            v_.tensor_tensor(fa[:, j, :], bank[2 * j][:, :], rbc[:, :], ALU.mult).then_inc(fa_ready, 1)
                            split(s4 + i, 2 * j + 1)
                            dve.wait_ge(slab_done, (s4 + i) * 4 + 2 * j + 2 + RING)
                            v_.tensor_tensor(fb[:, j, :], bank[2 * j + 1][:, :], rbc[:, :], ALU.mult).then_inc(ab_free, 1)
                            dve.wait_ge(ab_free, PI + 3)
                            dve.wait_ge(silu_ready, PI + 1)
                            v_.tensor_tensor(fb[:, j, :], fa[:, j, :], fb[:, j, :], ALU.mult).then_inc(h_ready, 1)
                            dve.wait_ge(hhi_ready, PI + 1)
                            m = bass.ds(i * 2 + j, 1)
                            v_.tensor_tensor(hlo[:, m, :], fb[:, j:j + 1, :], f32(hhi[:, m, :]), ALU.subtract).then_inc(hlo_ready, 1)
                    s4 = s4 + n // 2
                    with dve.Fori(0, KD // 4) as i:
                        for q in range(4):
                            split(s4 + i, q)
                            dve.wait_ge(slab_done, (s4 + i) * 4 + q + 1 + RING)
                            dve.wait_ge(x_done, xb + part * KD - KD + i * 4 + q + 1)
                            m = bass.ds(i * 4 + q, 1)
                            v_.scalar_tensor_tensor(out=xf[:, m, :], in0=bank[4 + q % 2][:, :].unsqueeze(1), scalar=0.5,
                                                    in1=xf[:, m, :], op0=ALU.mult, op1=ALU.add).then_inc(x_done, 1)
                    s4 = s4 + KD // 4

            def unit_taps(U, tile, lo, hi):
                for k in range(lo, hi):
                    if k == 0:
                        dve.wait_ge(unit_tap, U * DWK + 1)
                        src = prm[:, P_DW:P_CW].rearrange("p (k t) -> p k t", t=KD)[:, :, bass.ds(tile, 1)]
                        v_.tensor_scalar(cwg[:, :].unsqueeze(2), src, 0.5, None, ALU.mult).then_inc(cw_ready, 1)
                        dve.wait_ge(cw_ready, U + 1)
                        dve.wait_ge(vp_in, U * 16 + 16)
                        dve.wait_ge(c_out, U * 16 + 16)
                        v_.tensor_scalar(cacc[:, 0, :], vp[:, 0:SEQ], cwg[:, 0:1], prm[:, bass.ds(tile + P_DWB, 1)],
                                         ALU.mult, ALU.add).then_inc(unit_tap, 1)
                    elif k == 1:
                        v_.tensor_scalar(cacc[:, 1, :], vp[:, 1:1 + SEQ], cwg[:, 1:2], None, ALU.mult).then_inc(unit_tap, 1)
                    else:
                        dve.wait_ge(unit_tap, U * DWK + k)
                        v_.scalar_tensor_tensor(out=cacc[:, k % 2, :], in0=vp[:, k:k + SEQ], scalar=cwg[:, k:k + 1],
                                                in1=cacc[:, k % 2, :], op0=ALU.mult, op1=ALU.add).then_inc(unit_tap, 1)

            def unit_sum(U):
                dve.wait_ge(unit_tap, U * DWK + DWK + 1)
                v_.tensor_tensor(cacc[:, 0, :], cacc[:, 0, :], cacc[:, 1, :], ALU.add).then_inc(unit_done, 1)

            def group(L, g, slabs, ssd, norm):
                G = L * NG + g
                H, n = G - 1, G - 2
                s4 = L * (NSLAB // 4) + g * 2 + S_GROUP // 4
                U, tile = L * UNITS + g - 1, g - 1

                def conv(j):
                    t = j + 4
                    col = [g + 2 * KD, g + 3 * KD, g * 2, g * 2 + 1][j]
                    dve.wait_ge(pad_ready, G * 4 + j + 3)
                    if j == 0:
                        dve.wait_ge(yoff_ps, G * 2 + 1)
                        dve.wait_ge(xt_ps, G * 2 + 1)
                    base = G * 36 + 9 * j
                    for k in range(TAPS):
                        for r in range(2):
                            dst = bc[:, j, r * SEQ:(r + 1) * SEQ]
                            src = xpad[:, t % 2, r, k:k + SEQ]
                            w = prm[:, bass.ds(col + (P_CW + k * 4 * KD), 1)]
                            if k == 0:
                                ins = v_.tensor_scalar(dst, src, w, prm[:, bass.ds(col + P_CB, 1)], ALU.mult, ALU.add)
                            else:
                                dve.wait_ge(conv_tap, base + 2 * k + r)
                                ins = v_.scalar_tensor_tensor(out=dst, in0=src, scalar=w, in1=dst, op0=ALU.mult, op1=ALU.add)
                            ins.then_inc(cv_ready if (k, r) == (TAPS - 1, 1) else conv_tap, 1)

                def seg(c):
                    dve.wait_ge(seg_ps, H * NC + c + 2)
                    if c == 0:
                        dve.wait_ge(st_ps, H * 2 + 2)
                    e = E[:, c % 2].rearrange("p h i -> p (h i)")
                    v_.tensor_scalar(e, bank[2][:, :], 0.0, None, ALU.min).then_inc(seg_mid, 1)
                    dve.wait_ge(seg_mid, H * NC + c + 1)
                    v_.scalar_tensor_tensor(out=e, in0=bank[3][:, :], scalar=0.0, in1=e, op0=ALU.min, op1=ALU.add).then_inc(seg_ready, 1)

                def decays(c):
                    for h in range(HPG):
                        dve.wait_ge(t1_ready, (H * NC + c) * HPG + h + 1)
                        v_.scalar_tensor_tensor(out=TM[:, c % 2, h, :], in0=SUL[:, 0, c, :], scalar=dtg[:, c, 0, h:h + 1],
                                                in1=TM[:, c % 2, h, :], op0=ALU.mult, op1=ALU.add).then_inc(t2_ready, 1)
                    dve.wait_ge(t2_ready, (H * NC + c + 1) * HPG)
                    dve.wait_ge(e_ready, H * NC + c + 1)
                    v_.tensor_tensor(TM[:, c % 2], TM[:, c % 2], E[:, c % 2], ALU.mult).then_inc(m_ready, 1)

                def y_out_of_psum(c):
                    dve.wait_ge(y_ps, H * NC + c + 3)
                    dve.wait_ge(yt_ps, H * NC + c + 1)
                    dve.wait_ge(yoff_ready, H * 2 + 3)
                    v_.tensor_tensor(ytm[:, c % 2, :], bank[4][:, 0:GF], yoff[:, c, :], ALU.add).then_inc(y_ready, 1)

                def gating(c):
                    dve.wait_ge(yt_ps, H * NC + c + 3)
                    dve.wait_ge(xd_ready, H * 2 + 2)
                    dve.wait_ge(zcopied, H * 2 + 3)
                    v_.tensor_tensor(yz[:, :, chunk(c)], bank[5][:, 0:GF].rearrange("p (j i) -> p j i", j=2),
                                     yz[:, :, chunk(c)], ALU.add).then_inc(gate_mid, 1)
                    dve.wait_ge(gate_mid, H * NC + c + 1)
                    v_.tensor_tensor(yz[:, :, chunk(c)], yz[:, :, chunk(c)], zcur[:, :, chunk(c)], ALU.mult).then_inc(gated, 1)

                for t in range(8):
                    if slabs:
                        split(s4 + t // 4, t % 4)
                    if ssd and 3 <= t < 7:
                        decays(t - 3)
                    if ssd and t < len(TAP_SLICES):
                        unit_taps(U, tile, *TAP_SLICES[t])
                    if ssd and t == len(TAP_SLICES):
                        unit_sum(U)
                    if t == 0 and ssd:
                        dve.wait_ge(sc_ps, H + 1)
                        for d in range(2):
                            v_.tensor_tensor(SUL[:, d], bank[5][:, :].rearrange("p (c i) -> p c i", c=NC),
                                             ul[:, d, :].unsqueeze(1).broadcast_to([P, NC, P]), ALU.mult).then_inc(sul_ready, 1)
                        dve.wait_ge(xt_ready, H * 2 + 2)
                        dve.wait_ge(small_ready, H * 5 + 5)
                        v_.tensor_tensor(xw[:, :, :].rearrange("p c (h e) -> p (c h) e", h=HPG),
                                         xT[:, :, :].rearrange("p c (h e) -> p (c h) e", h=HPG),
                                         wg[:, :, :].rearrange("p c h -> p (c h)").unsqueeze(2).broadcast_to([P, NC * HPG, HEAD]),
                                         ALU.mult).then_inc(xw_ready, 1)
                    if t == 1 and slabs:
                        dve.wait_ge(slab_done, (s4 * 4) + 2 + RING)
                        dve.wait_ge(tg_ready, G + 1)
                        v_.scalar_tensor_tensor(out=tg[:, :], in0=tg[:, :], scalar=1.0, in1=bank[1][:, :],
                                                op0=ALU.add, op1=ALU.mult).then_inc(v_ready, 1)
                    if t == 2 and norm:
                        dve.wait_ge(gr_ready, n + 1)
                        for j in range(2):
                            v_.scalar_tensor_tensor(out=yz[:, j, :], in0=yz[:, j, :],
                                                    scalar=prm[:, bass.ds(g * 2 + (P_SN - 4 + j), 1)], in1=rg[:, :],
                                                    op0=ALU.mult, op1=ALU.mult).then_inc(y2_ready, 1)
                    if t == 2 and ssd:
                        for b in range(2):
                            dve.wait_ge(yoff_ps, H * 2 + b + 2)
                            v_.tensor_tensor(yoff[:, 2 * b:2 * b + 2, :].rearrange("p c (h e) -> p (c h) e", h=HPG),
                                             bank[6 + b][:, :].rearrange("p (x e) -> p x e", e=HEAD),
                                             exg[:, 2 * b:2 * b + 2, :].rearrange("p c h -> p (c h)").unsqueeze(2).broadcast_to([P, 2 * HPG, HEAD]),
                                             ALU.mult).then_inc(yoff_ready, 1)
                    if t == 3 and ssd:
                        dve.wait_ge(y_out, H * 16 + 16)
                        dve.wait_ge(bc_ready, H * 4 + 4)
                        for j in range(2):
                            v_.tensor_scalar(yz[:, j, :], bc[:, 2 + j, :], dskip[:, bass.ds(L * XT_ + g * 2 + (j - 2), 1)], None,
                                             ALU.mult).then_inc(xd_ready, 1)
                    if ssd and t >= 4:
                        gating(t - 4)
                    if ssd and 2 <= t < 6:
                        seg(t - 2)
                    if ssd and 3 <= t < 7:
                        y_out_of_psum(t - 3)
                    if slabs and t >= 4:
                        conv(t - 4)

            with dve.Fori(0, DEPTH) as L:
                dve.wait_ge(prm2_ready, 2 * DEPTH + 2)
                src = prm2[:, bass.ds(L, 1), :]
                v_.tensor_copy(prm[:, :].unsqueeze(1), src).then_inc(prm_ready, 1)
                v_.tensor_scalar(hbias[:, :].unsqueeze(1), src[:, :, P_GBIAS:P_GBIAS + 2 * KD], 0.5, None, ALU.mult).then_inc(prm_ready, 1)
                dve.wait_ge(prm_ready, L * 2 + 2)
                ffn(L, 0, 0)
                dve.wait_ge(wd_hi_ready, L + 1)
                v_.tensor_tensor(wd_lo[:, :, :], wd_raw[:, :, :], f32(wd_hi[:, :, :]), ALU.subtract).then_inc(wd_lo_ready, 1)
                N = L * 3 + 1
                dve.wait_ge(r_ready, N + 1)
                for k in range(KD + 1):
                    if k < KD:
                        dve.wait_ge(u_ready, N * KD + k - 1)
                        v_.scalar_tensor_tensor(out=sq[:, k % 2, :], in0=xf[:, k, :], scalar=prm[:, P_MIX + k:P_MIX + k + 1],
                                                in1=rbc[:, :], op0=ALU.mult, op1=ALU.mult).then_inc(nt_ready, 1)
                    if k:
                        dve.wait_ge(nhi_ready, N * KD + k)
                        v_.tensor_tensor(ulo[:, k - 1, :], sq[:, (k - 1) % 2, :], f32(uhi[:, k - 1, :]), ALU.subtract).then_inc(u_ready, 1)
                d0 = L * ND
                dve.wait_ge(dt_ps, L + 1)
                v_.tensor_scalar(dx[:, :], bank[0][0:2 * NH, :], dtbA[:, 0, bass.ds(L, 1)], None, ALU.add).then_inc(dt_dve, 1)
                dve.wait_ge(dt_act, L * 5 + 2)
                v_.tensor_scalar(du[:, :], de[:, :], 1.0, None, ALU.add).then_inc(dt_dve, 1)
                dve.wait_ge(dt_dve, d0 + 2)
                v_.tensor_scalar(dc[:, :], du[:, :], -1.0, None, ALU.add).then_inc(dt_dve, 1)
                dve.wait_ge(dt_dve, d0 + 3)
                v_.tensor_tensor(dc[:, :], de[:, :], dc[:, :], ALU.subtract).then_inc(dt_dve, 1)
                dve.wait_ge(dt_dve, d0 + 4)
                v_.reciprocal(de[:, :], du[:, :]).then_inc(dt_dve, 1)
                dve.wait_ge(dt_dve, d0 + 5)
                v_.tensor_tensor(dc[:, :], dc[:, :], de[:, :], ALU.mult).then_inc(dt_dve, 1)
                v_.tensor_scalar(dx[:, :], dx[:, :], 0.0, None, ALU.max).then_inc(dt_dve, 1)
                dve.wait_ge(dt_dve, d0 + 7)
                v_.tensor_tensor(dx[:, :], dx[:, :], dc[:, :], ALU.add).then_inc(dt_dve, 1)
                dve.wait_ge(dt_dve, d0 + 8)
                dve.wait_ge(dt_act, L * 5 + 3)
                v_.tensor_tensor(dtf[:, 0, :], dx[:, :], dl[:, :], ALU.add).then_inc(dt_dve, 1)
                dve.wait_ge(dt_dve, d0 + 9)
                v_.tensor_scalar(dtf[:, 1, :], dtf[:, 0, :], negA[:, bass.ds(L, 1)], None, ALU.mult).then_inc(dt_dve, 1)
                for b in range(2):
                    for d in range(2):
                        dve.wait_ge(rt_hi, L * 4 + 2 * b + d + 1)
                        rows = slice(d * NH, (d + 1) * NH)
                        low = slice((2 + d) * NH, (3 + d) * NH)
                        src = bank[2 + b][rows, :].rearrange("p (c d i) -> p c d i", c=2, d=2)[:, :, d, :]
                        v_.tensor_tensor(rt[low, 2 * b:2 * b + 2, :], src, f32(rt[rows, 2 * b:2 * b + 2, :]), ALU.subtract).then_inc(rt_ready, 1)
                dve.wait_ge(dt_act, L * 5 + 4)
                v_.tensor_tensor(ddS[:, :, :], bank[4][:, 256:512].rearrange("p (c x) -> p c x", c=NC), cumS[:, :, :], ALU.subtract).then_inc(dt_dve, 1)
                dve.wait_ge(dt_act, L * 5 + 5)
                dve.wait_ge(dtr_ev, L * 2 + 2)
                v_.tensor_tensor(wT[:, :, :], dtT[:, :, :], ddS[:, :, :], ALU.mult).then_inc(wT_ready, 1)
                v_.memset(xpad[:, :, :, :], 0.0).then_inc(pad_zero, 1)
                group(L, 0, True, False, False)
                group(L, 1, True, True, False)
                with dve.Fori(2, NG) as g:
                    group(L, g, True, True, True)
                group(L, NG, False, True, True)
                group(L, NG + 1, False, False, True)
                for k in range(XT_):
                    dve.wait_ge(yhi_ready, L * XT_ + k + 1)
                    hi, lo = (hhi, hlo) if k < KD else (phi, plo)
                    v_.tensor_tensor(lo[:, k % KD, :], yraw[:, k % 4, :], f32(hi[:, k % KD, :]), ALU.subtract).then_inc(y_split, 1)
                s4 = L * (NSLAB // 4)
                slices = [(0, 8), (8, 16), (16, 24), (24, DWK)]
                with dve.Fori(0, KD // 2) as i:
                    for q in range(4):
                        split(s4 + S_SSDO // 4 + i, q)
                        unit_taps(L * UNITS + KD + i, i, *slices[q])
                    unit_sum(L * UNITS + KD + i)
                with dve.Fori(0, KD // 4) as i:
                    for q in range(4):
                        split(s4 + S_GB // 4 + i, q)
                        unit_taps(L * UNITS + KD + KD // 2 + i, i + KD // 2, *slices[q])
                        dve.wait_ge(gt_free, L * 2 * KD + i * 4 + q + 3)
                        dve.wait_ge(so_free, L * KD + i * 4 + q + 3)
                        m = bass.ds(i * 4 + q, 1)
                        v_.scalar_tensor_tensor(out=mix[:, m, :], in0=mtmp[:, q % 2:q % 2 + 1, :], scalar=1.0, in1=mix[:, m, :],
                                                op0=ALU.add, op1=ALU.mult).then_inc(mix_b, 1)
                    unit_sum(L * UNITS + KD + KD // 2 + i)
                with dve.Fori(0, KD // 4) as i:
                    for q in range(4):
                        split(s4 + S_GA // 4 + i, q)
                        unit_taps(L * UNITS + KD + 3 * KD // 4 + i, i + 3 * KD // 4, *slices[q])
                    unit_sum(L * UNITS + KD + 3 * KD // 4 + i)
                dve.wait_ge(mu_ready, L + 1)
                for k in range(KD):
                    v_.tensor_tensor(cv[:, k, :], cv[:, k, :], mu[:, :], ALU.subtract).then_inc(d_ready, 1)
                dve.wait_ge(lr_ready, L + 1)
                for k in range(KD):
                    v_.tensor_tensor(cv[:, k, :], cv[:, k, :], rstd[:, :], ALU.mult).then_inc(n_ready, 1)
                for k in range(KD):
                    dve.wait_ge(chi_ready, L * KD + k + 1)
                    v_.tensor_tensor(hlo[:, k, :], cv[:, k, :], f32(hhi[:, k, :]), ALU.subtract).then_inc(c_split, 1)
                with dve.Fori(0, KD // 4) as i:
                    for q in range(4):
                        idx = L * KD + i * 4 + q
                        split(s4 + S_CONF // 4 + i, q)
                        dve.wait_ge(slab_done, (s4 + i) * 4 + (S_CONF + q + 1) + RING)
                        m = bass.ds(i * 4 + q, 1)
                        v_.scalar_tensor_tensor(out=mtmp[:, q % 2:q % 2 + 1, :], in0=ga[:, m, :], scalar=1.0,
                                                in1=bank[q % 2][:, :].unsqueeze(1), op0=ALU.add, op1=ALU.mult).then_inc(ya_mid, 1)
                        dve.wait_ge(ya_mid, idx + 3)
                        dve.wait_ge(mix_b, idx + 3)
                        v_.tensor_tensor(mix[:, m, :], mix[:, m, :], mtmp[:, q % 2:q % 2 + 1, :], ALU.add).then_inc(mix_ready, 1)
                        dve.wait_ge(mhi_ready, idx + 1)
                        v_.tensor_tensor(ulo[:, m, :], mix[:, m, :], f32(uhi[:, m, :]), ALU.subtract).then_inc(m_split, 1)
                with dve.Fori(0, KD // 4) as i:
                    for q in range(4):
                        split(s4 + S_WO // 4 + i, q)
                        dve.wait_ge(slab_done, (s4 + i) * 4 + (S_WO + q + 1) + RING)
                        dve.wait_ge(x_done, L * XL + X_WO + i * 4 + q + 1)
                        m = bass.ds(i * 4 + q, 1)
                        v_.scalar_tensor_tensor(out=xf[:, m, :], in0=bank[2 + q % 2][:, :].unsqueeze(1), scalar=0.5,
                                                in1=xf[:, m, :], op0=ALU.mult, op1=ALU.add).then_inc(x_done, 1)
                ffn(L, 1, S_FFN2)
            dve.wait_ge(r_ready, 3 * DEPTH + 1)
            for k in range(KD):
                v_.scalar_tensor_tensor(out=yfin[:, k, :], in0=xf[:, k, :], scalar=prm2[:, 0, P_FIN + k:P_FIN + k + 1],
                                        in1=rbc[:, :], op0=ALU.mult, op1=ALU.mult).then_inc(fin_ready, 1)

        @block.tensor
        def _(pe):
            t_ = nc.tensor

            def three(out, slot, k0, nk, hi, lo, start, stop):
                for k in range(nk):
                    w = slice((k0 + k) * P, (k0 + k + 1) * P)
                    for a, b in ((whi, hi), (whi, lo), (wlo, hi)):
                        ins = t_.matmul(out, a[:, slot, w], b[:, k, :], start=start and k == 0 and a is whi and b is hi,
                                        stop=stop and k == nk - 1 and a is wlo)
                return ins

            def slab(s, q, out, hi, lo, nk=8, start=True, stop=True):
                pe.wait_ge(lo_ready, s + 1 + RING)
                three(out, q, 0, nk, hi, lo, start, stop).then_inc(slab_done, 1)

            pe.wait_ge(const_fix, 7)
            pe.wait_ge(x_in, 32)
            for m in range(KD):
                if m >= 2:
                    pe.wait_ge(x_done, m - 1)
                for c in range(NC):
                    ins = t_.transpose(bank[m % 2][:, chunk(c)], x_tm[:, c, m * P:(m + 1) * P], ident[:, :])
                ins.then_inc(x_ps, 1)
            pe.wait_ge(consts_in, NCONST * 16)
            pe.wait_ge(v_out, 16)
            pe.wait_ge(y_out, 16)
            pe.wait_ge(c_out, 16)
            for l in range(DEPTH):
                col = 0
                for b, rows in enumerate(BROWS):
                    if b == len(BROWS) - 1:
                        ins.then_inc(prm_ps, 1)
                        col = 0
                    ins = t_.transpose(bank[2 + 2 * l + (b == len(BROWS) - 1)][:, col:col + rows],
                                       stage[0:rows, 5 * l + b, :], ident[0:rows, 0:rows])
                    col += rows
                ins.then_inc(prm_ps, 1)

            def stats(N):
                for k in range(KD):
                    pe.wait_ge(sq_ready, N * KD + k + 1)
                    t_.matmul(bank[6][:, :], ones[:, :], sq[:, k % 2, :], start=k == 0, stop=k == KD - 1).then_inc(stat_mm, 1)

            def ffn(L, f, base):
                N = L * 3 + 2 * f
                xb = L * XL + (KD if f == 0 else X_WO + 2 * KD)
                stats(N)
                pe.wait_ge(u_ready, N * KD + KD)
                pe.sem_inc(pe_passed, 1)
                s = L * NSLAB + base
                for part, (p0, n) in enumerate(PARTS):
                    with pe.Fori(0, n // 2) as i:
                        for j in range(2):
                            PI = L * (2 * FT) + (f * FT + p0 + j) + i * 2
                            pe.wait_ge(ab_free, PI + 1)
                            slab(s + i * 4 + 2 * j, 2 * j, bank[2 * j][:, :], uhi, ulo)
                            slab(s + i * 4 + 2 * j + 1, 2 * j + 1, bank[2 * j + 1][:, :], uhi, ulo)
                    s = s + 2 * n
                    pe.wait_ge(hlo_ready, L * (2 * FT) + (f * FT + p0 + n))
                    pe.sem_inc(pe_passed, 1)
                    with pe.Fori(0, KD // 4) as i:
                        for q in range(4):
                            pe.wait_ge(x_done, xb + part * KD + i * 4 + q - 1)
                            slab(s + i * 4 + q, q, bank[4 + q % 2][:, :], hhi, hlo, nk=n)
                    s = s + KD

            def group(L, g, slabs, ssd, norm):
                G = L * NG + g
                H, n = G - 1, G - 2
                s = L * NSLAB + g * 8 + S_GROUP

                def seg(c):
                    pe.wait_ge(seg_ready, H * NC + c + 1)
                    for d in range(2):
                        out = bank[2 + d][:, :]
                        t_.matmul(out.rearrange("p (h i) -> p h i", h=HPG), rt[:, c, :],
                                  selg[:, 1, d, :].unsqueeze(2).broadcast_to([P, HPG, P]), start=True, stop=False,
                                  skip_group_check=True)
                        for h in range(HPG):
                            ins = t_.matmul(out[:, chunk(h)], selg[:, 0, d, h:h + 1].broadcast_to([P, P]), rt[:, c, :],
                                            start=False, stop=h == HPG - 1, skip_group_check=True)
                    ins.then_inc(seg_ps, 1)

                free = [(pad_ready, G * 4 + 1), (pad_ready, G * 4 + 2), (tg_ready, G + 1), (v_ready, G + 1),
                        (z_ready, G * 2 + 1), (z_ready, G * 2 + 2), (pad_ready, G * 4 + 3), (pad_ready, G * 4 + 4)]
                for t in range(8):
                    if slabs:
                        pe.wait_ge(*free[t])
                        slab(s + t, t % RING, bank[t % 2][:, :], uhi, ulo)
                    if t == 0 and ssd:
                        pe.wait_ge(bc_ready, H * 4 + 4)
                        pe.wait_ge(seg_ready, H * NC + 1)
                        for c in range(NC):
                            for j in range(2):
                                ins = t_.transpose(bank[2 + c // 2][:, (c % 2) * GF + j * P:(c % 2) * GF + (j + 1) * P],
                                                   bc[:, 2 + j, chunk(c)], ident[:, :])
                            if c % 2:
                                ins.then_inc(xt_ps, 1)
                        pe.wait_ge(y_ready, H * NC + 1)
                        for c in range(NC):
                            ins = t_.transpose(bank[4][:, chunk(c)], bc[:, 0, chunk(c)], ident[:, :])
                        ins.then_inc(bt_ps, 1)
                        pe.wait_ge(gated, H * NC + 1)
                        for c in range(NC):
                            ins = t_.matmul(bank[5][:, chunk(c)], bc[:, 0, chunk(c)], bc[:, 1, chunk(c)], start=True, stop=True)
                        ins.then_inc(sc_ps, 1)
                    if t == 1 and ssd:
                        pe.wait_ge(xw_ready, H + 2)
                        pe.wait_ge(bt_ready, H + 1)
                        pe.wait_ge(yoff_ready, H * 2 + 1)
                        for c in range(NC):
                            ins = t_.matmul(bank[6 + c // 2][:, (c % 2) * GF:(c % 2 + 1) * GF], bT[:, c, :], xw[:, c, :], start=True, stop=True)
                            if c % 2:
                                ins.then_inc(st_ps, 1)
                    if t == 1 and norm:
                        pe.wait_ge(gsq, n * 2 + 2)
                        for j in range(2):
                            ins = t_.matmul(bank[4][:, :], ones[:, :], sq[:, j, :], start=j == 0, stop=j == 1)
                        ins.then_inc(gst_ps, 1)
                    if t == 2 and ssd:
                        pe.wait_ge(st_ready, H * 2 + 2)
                        for c in range(NC):
                            ins = t_.matmul(bank[6 + c // 2][:, (c % 2) * GF:(c % 2 + 1) * GF], bc[:, 1, chunk(c)],
                                            st[:, c ^ 1, :], start=True, stop=True)
                            if c % 2:
                                ins.then_inc(yoff_ps, 1)
                        pe.wait_ge(small_ready, H * 5 + 5)
                        pe.wait_ge(rt_ready, L * 4 + 4)
                    if ssd and t >= 4:
                        c = t - 4
                        pe.wait_ge(y_ready, H * NC + c + 2)
                        pe.wait_ge(gated, H * NC + c + 1)
                        for j in range(2):
                            ins = t_.transpose(bank[5][:, j * P:(j + 1) * P], ytm[:, c % 2, j * P:(j + 1) * P], ident[:, :])
                        ins.then_inc(yt_ps, 1)
                    if ssd and 3 <= t < 7:
                        c = t - 3
                        if c == 0 and norm:
                            pe.wait_ge(gln, n + 1)
                        pe.wait_ge(m_ready, H * NC + c + 2)
                        pe.wait_ge(y_ready, H * NC + c + 1)
                        for h in range(HPG):
                            ins = t_.matmul(bank[4][:, h * HEAD:(h + 1) * HEAD], TM[:, c % 2, h, :],
                                            xT[:, c, h * HEAD:(h + 1) * HEAD], start=True, stop=True)
                        ins.then_inc(y_ps, 1)
                    if ssd and 2 <= t < 6:
                        seg(t - 2)

            with pe.Fori(0, DEPTH) as L:
                ffn(L, 0, 0)
                stats(L * 3 + 1)
                pe.wait_ge(u_ready, L * 3 * KD + 2 * KD)
                pe.wait_ge(wd_lo_ready, L + 1)
                for k in range(KD):
                    for a, b in ((wd_hi, uhi), (wd_hi, ulo), (wd_lo, uhi)):
                        ins = t_.matmul(bank[0][:, :], a[:, k, :], b[:, k, :], start=k == 0 and a is wd_hi and b is uhi,
                                        stop=k == KD - 1 and a is wd_lo)
                ins.then_inc(dt_ps, 1)
                pe.wait_ge(dt_dve, L * ND + 10)
                pe.sem_inc(pe_passed, 1)
                for j in range(2):
                    for c in range(NC):
                        ins = t_.transpose(bank[1][:, (j * NC + c) * 2 * NH:(j * NC + c + 1) * 2 * NH], dtf[:, j, chunk(c)], ident[0:2 * NH, 0:2 * NH])
                ins.then_inc(dtr_ps, 1)
                pe.wait_ge(dtr_ev, L * 2 + 2)
                for c in range(NC):
                    ins = t_.matmul(bank[2 + c // 2][0:2 * NH, (c % 2) * 2 * P:(c % 2 + 1) * 2 * P], aT[:, c, :],
                                    ul[:, :, :].rearrange("p d i -> p (d i)"), start=True, stop=True)
                ins.then_inc(rt_ps, 1)
                cum = bank[4][:, 0:256].rearrange("p (c x) -> p c x", c=NC)
                for d in range(2):
                    t_.matmul(cum[:, :, d * NH:(d + 1) * NH], ul[:, d, :], aT[:, :, d * NH:(d + 1) * NH], start=True, stop=True)
                t_.matmul(bank[4][:, 256:512], ones[:, :], aT[:, :, :].rearrange("p c x -> p (c x)"), start=True, stop=True).then_inc(cum_ps, 1)
                group(L, 0, True, False, False)
                group(L, 1, True, True, False)
                with pe.Fori(2, NG) as g:
                    group(L, g, True, True, True)
                group(L, NG, False, True, True)
                group(L, NG + 1, False, False, True)
                s = L * NSLAB
                pe.wait_ge(y_split, L * XT_ + XT_ + 4)
                pe.sem_inc(pe_passed, 1)
                with pe.Fori(0, KD // 2) as i:
                    for q in range(4):
                        if q % 2 == 0:
                            pe.wait_ge(so_free, L * KD + i * 2 + q // 2 + 1)
                        hi, lo = (phi, plo) if q % 2 else (hhi, hlo)
                        slab(s + i * 4 + (S_SSDO + q), q, bank[2 + q // 2][:, :], hi, lo, start=q % 2 == 0, stop=q % 2 == 1)
                for j, base in enumerate((S_GB, S_GA)):
                    with pe.Fori(0, KD // 4) as i:
                        for q in range(4):
                            pe.wait_ge(gt_free, L * 2 * KD + i * 4 + (j * KD + q - 1) + 2)
                            slab(s + i * 4 + (base + q), q, bank[4 + q % 2][:, :], uhi, ulo)
                pe.wait_ge(cv_in, L * 32 + 32)
                for k in range(KD):
                    ins = t_.matmul(bank[6][:, :], ones[:, :], cv[:, k, :], start=k == 0, stop=k == KD - 1)
                ins.then_inc(mu_ps, 1)
                for k in range(KD):
                    pe.wait_ge(lsq, L * KD + k + 1)
                    t_.matmul(bank[7][:, :], ones[:, :], sq[:, k % 2, :], start=k == 0, stop=k == KD - 1).then_inc(lst_ps, 1)
                pe.wait_ge(c_split, L * KD + KD)
                pe.sem_inc(pe_passed, 1)
                with pe.Fori(0, KD // 4) as i:
                    for q in range(4):
                        pe.wait_ge(ya_mid, L * KD + i * 4 + q + 1)
                        slab(s + i * 4 + (S_CONF + q), q, bank[q % 2][:, :], hhi, hlo)
                pe.wait_ge(m_split, L * KD + KD)
                pe.sem_inc(pe_passed, 1)
                with pe.Fori(0, KD // 4) as i:
                    for q in range(4):
                        pe.wait_ge(x_done, L * XL + (X_WO + KD - 1) + i * 4 + q)
                        slab(s + i * 4 + (S_WO + q), q, bank[2 + q % 2][:, :], uhi, ulo)
                ffn(L, 1, S_FFN2)
            stats(3 * DEPTH)
            pe.wait_ge(fin_ready, KD)
            for c in range(NC):
                for half in range(2):
                    b = 2 * c + half
                    if b >= 4:
                        pe.wait_ge(out_ready, b - 3)
                    for k in range(4):
                        ins = t_.transpose(bank[b % 4][:, chunk(k)], yfin[:, half * 4 + k, chunk(c)], ident[:, :])
                    ins.then_inc(out_ps, 1)


_INS = ["x_prompt", "x_sample", "ffn1_norm", "ffn1_w_up", "ffn1_w_down", "mix_norm", "w_in", "gate_bias",
        "conf_dw_w", "conf_dw_b", "conf_ln_g", "conf_ln_b", "conf_w_out", "ssd_conv_w", "ssd_conv_b",
        "ssd_dt_bias", "ssd_A_log", "ssd_D", "ssd_norm", "ssd_w_out", "w_o", "ffn2_norm", "ffn2_w_up",
        "ffn2_w_down", "final_norm"]


def kernel(**inputs):
    import numpy as _np
    import concourse.bacc as _bacc
    from concourse import mybir as _mybir
    from concourse.bass_utils import run_bass_kernel_spmd as _run

    nc = _bacc.Bacc("TRN2", target_bir_lowering=False, num_devices=1)
    arrays, io = {}, {}
    for name in _INS:
        a = _np.ascontiguousarray(inputs[name])
        arrays[f"in_{name}"] = a
        io[name] = nc.dram_tensor(f"in_{name}", a.shape, _mybir.dt.from_np(a.dtype), kind="ExternalInput").ap()
    for i, name in enumerate(("x_prompt", "x_sample")):
        a = arrays[f"in_{name}"]
        io[f"out_{i}"] = nc.dram_tensor(f"out_{i}", a.shape, _mybir.dt.from_np(a.dtype), kind="ExternalOutput").ap()
    trunk(nc, io)
    r = _run(nc, [arrays], core_ids=[0])
    return tuple(r.results[0][f"out_{i}"] for i in range(2))
```

```python
from contextlib import ExitStack

import concourse.bass as bass
from concourse import mybir

F32 = mybir.dt.float32
F32R = mybir.dt.float32r
ALU = mybir.AluOpType
ACT = mybir.ActivationFunctionType

P = 128
RING = 4
AHEAD = 3
EPS = 1e-6
BIG = 1e9
HEAD = 64
HPG = 4
TAPS = 5


def trunk(nc, io):
    x_prompt, x_sample = io["x_prompt"], io["x_sample"]
    SEQ, DM = x_prompt.shape[1:]
    DEPTH = io["w_in"].shape[0]
    FF = io["ffn1_w_down"].shape[1]
    DWK = io["conf_dw_w"].shape[1]
    HALO = DWK // 2
    T = 2 * SEQ
    KD = DM // P
    FT = FF // P
    NG = KD
    XT_ = 2 * KD
    NH = NG * HPG
    GF = HPG * HEAD
    NC = T // P
    CPR = SEQ // P
    assert T == 512 and CPR == 2 and DM == 1024 and DWK == 31
    C_A, C_GATE, C_Z = 0, DM, 2 * DM
    C_X = C_Z + 2 * DM
    C_B = C_X + 2 * DM
    C_C = C_B + DM
    C_DT = C_C + DM
    C_GA = C_DT + 2 * NH
    C_GB = C_GA + DM
    PARTS = [(0, 8), (8, 8), (16, FT - 16)]
    FFN_SLABS = 2 * FT + KD * len(PARTS)
    S_GROUP = FFN_SLABS
    S_GB = S_GROUP + 8 * NG
    S_GA = S_GB + KD
    S_SSDO = S_GA + KD
    S_CONF = S_SSDO + 2 * KD
    S_WO = S_CONF + KD
    S_FFN2 = S_WO + KD
    NSLAB = S_FFN2 + FFN_SLABS
    assert all(s % RING == 0 for s in (S_GROUP, S_SSDO, S_GB, S_GA, S_CONF, S_WO, S_FFN2, NSLAB))

    P_FFN1, P_MIX, P_FFN2, P_FIN = 0, KD, 2 * KD, 3 * KD
    P_LNG, P_LNB, P_DWB, P_SN = 4 * KD, 5 * KD, 6 * KD, 7 * KD
    P_CB = P_SN + XT_
    P_GBIAS = P_CB + 4 * KD
    P_DW = P_GBIAS + 2 * KD
    P_CW = P_DW + DWK * KD
    NPRM = P_CW + TAPS * 4 * KD

    BROWS = [P_DW, P, DWK * KD - P, P, TAPS * 4 * KD - P]
    PB = sum(BROWS[:-1])
    NCONST = 11 + 3 * DEPTH
    ND, NA = 16, 6
    NB = NC // 2

    v_dram = nc.dram_tensor("v_spill", [2, KD, P, SEQ], F32, kind="Internal").ap()
    c_dram = nc.dram_tensor("conv_spill", [2, KD, P, SEQ], F32, kind="Internal").ap()
    y_dram = nc.dram_tensor("y_spill", [XT_, P, T], F32, kind="Internal").ap()

    kview = lambda w: w.rearrange("l (k p) f -> p (l k) f", p=P)
    W_UP = [kview(io["ffn1_w_up"]), kview(io["ffn2_w_up"])]
    W_DOWN = [kview(io["ffn1_w_down"]), kview(io["ffn2_w_down"])]
    W_IN, W_CONF, W_SSD, W_O = (kview(io[n]) for n in ("w_in", "conf_w_out", "ssd_w_out", "w_o"))

    with ExitStack() as ctx:
        def sb(name, shape, dt=F32, at=ctx):
            return at.enter_context(nc.sbuf_tensor(name, shape, dt))

        def sem(name):
            return ctx.enter_context(nc.semaphore(name))

        xf = sb("xf", [P, KD, T])
        wraw = sb("wraw", [P, RING, 8 * P])
        whi = sb("whi", [P, RING, 8 * P], F32R)
        wlo = sb("wlo", [P, RING, 8 * P], F32R)
        uhi = sb("uhi", [P, KD, T], F32R)
        ulo = sb("ulo", [P, KD, T], F32R)
        ident = sb("ident", [P, P])
        ones = sb("ones", [P, P])
        ul = sb("ul", [P, 2, P])
        selr = sb("selr", [P, 2, 2 * NH])
        identr = sb("identr", [P, P], F32R)
        never = sb("never", [P, 2, P], F32R)
        prm2 = sb("prm2", [P, DEPTH, NPRM])
        prm = sb("prm", [P, NPRM])
        rbc = sb("rbc", [P, T])
        sq = sb("sq", [P, 2, T])
        acc = sb("acc", [P, T])
        dskip = sb("dskip", [P, DEPTH * XT_])
        dtbA = sb("dtbA", [2 * NH, 2, DEPTH])
        negA = sb("negA", [2 * NH, DEPTH])
        hbias = sb("hbias", [P, 2 * KD])
        eps_t = sb("eps_t", [P, 1])

        with ExitStack() as s0:
            stage = sb("stage", [P, DEPTH * 5, P], at=s0)
            x_tm = sb("x_tm", [P, NC, DM], at=s0)
            dall = sb("dall", [P, DEPTH, NH], at=s0)
            neverf = sb("neverf", [P, 2, P], at=s0)
        with ExitStack() as s5:
            yfin = sb("yfin", [P, KD, T], at=s5)
            o_tm = sb("o_tm", [P, NC, DM], at=s5)
        with ExitStack() as s2:
            wd_raw = sb("wd_raw", [P, 8, P], at=s2)
            wd_hi = sb("wd_hi", [P, 8, P], F32R, at=s2)
            wd_lo = sb("wd_lo", [P, 8, P], F32R, at=s2)
            dx = sb("dx", [2 * NH, T], at=s2)
            de = sb("de", [2 * NH, T], at=s2)
            du = sb("du", [2 * NH, T], at=s2)
            dl = sb("dl", [2 * NH, T], at=s2)
            dc = sb("dc", [2 * NH, T], at=s2)
            dtf = sb("dtf", [2 * NH, 2, T], at=s2)
            aT = sb("aT", [P, NC, 2 * NH], at=s2)
            cumS = sb("cumS", [P, NC, 2 * NH], at=s2)
            ddS = sb("ddS", [P, NC, 2 * NH], at=s2)
        mix = sb("mix", [P, KD, T])
        with ExitStack() as s3:
            E = sb("E", [P, NC, 2, HPG * P], at=s3)
        ga = sb("ga", [P, KD, T])
        with ExitStack() as s3:
            tg = sb("tg", [P, T], at=s3)
            xpad = sb("xpad", [P, 2, 2, SEQ + TAPS - 1], at=s3)
            bc = sb("bc", [P, 4, T], at=s3)
            znew = sb("znew", [P, 2, T], at=s3)
            xT = sb("xT", [P, NC, GF], at=s3)
            SC = sb("SC", [P, NC, P], at=s3)
            bT = sb("bT", [P, NC, P], at=s3)
            ytm = sb("ytm", [P, 2, GF], at=s3)
            dtT = sb("dtT", [P, NC, 2 * NH], at=s3)
            exT = sb("exT", [P, NC, 2 * NH], at=s3)
            wT = sb("wT", [P, NC, 2 * NH], at=s3)
        hhi = sb("hhi", [P, KD, T], F32R)
        hlo = sb("hlo", [P, KD, T], F32R)
        with ExitStack() as s1:
            fa = sb("fa", [P, 2, T], at=s1)
            fb = sb("fb", [P, 2, T], at=s1)
        with ExitStack() as s3:
            yz = sb("yz", [P, 2, T], at=s3)
            rg = sb("rg", [P, T], at=s3)
        mtmp = sb("mtmp", [P, 2, T])
        mu = sb("mu", [P, T])
        with ExitStack() as s3:
            xw = sb("xw", [P, NC, GF], at=s3)
            zcur = sb("zcur", [P, 2, T], at=s3)
            yoff = sb("yoff", [P, NC, GF], at=s3)
            vp = sb("vp", [P, 2, SEQ + 2 * HALO], at=s3)
            cacc = sb("cacc", [P, 2, T], at=s3)
            rt = sb("rt", [P, NC, P], F32R, at=s3)
            rtm = sb("rtm", [P, NC, P], F32R, at=s3)
            exg = sb("exg", [P, NC, HPG], at=s3)
            wg = sb("wg", [P, NC, HPG], at=s3)
            selg = sb("selg", [P, 2, 2, HPG], F32R, at=s3)
            cwg = sb("cwg", [P, DWK], at=s3)
        with ExitStack() as s4:
            yraw = sb("yraw", [P, 4, T], at=s4)
        cv = sb("cv", [P, KD, T])
        phi, plo = uhi, ulo

        bank = [ctx.enter_context(nc.psum_tensor(f"bank{i}", [P, 512], F32)) for i in range(8)]

        pool_passed, pe_passed, dve_passed = (sem(n) for n in "pool_passed pe_passed dve_passed".split())
        raw_in = [sem(f"raw_in{i}") for i in range(RING)]
        yr_in = [sem(f"yr_in{i}") for i in range(4)]
        hi_ready, lo_ready, slab_done = (
            sem(n) for n in "hi_ready lo_ready slab_done".split())
        consts_in, const_made, const_fix, x_in, prm_ps, prm2_ready, negA_exp, negA_ready = (
            sem(n) for n in "consts_in const_made const_fix x_in prm_ps prm2_ready negA_exp negA_ready".split())
        prm_ready, x_ps, x_done = (
            sem(n) for n in "prm_ready x_ps x_done".split())
        sq_ready, sq_added, stat_mm, lnr, r_ready, nt_ready, nhi_ready, u_ready = (
            sem(n) for n in "sq_ready sq_added stat_mm lnr r_ready nt_ready nhi_ready u_ready".split())
        ab_free, fa_ready, silu_ready, h_ready, hhi_ready, hlo_ready = (
            sem(n) for n in "ab_free fa_ready silu_ready h_ready hhi_ready hlo_ready".split())
        wd_in, wd_hi_ready, wd_lo_ready, dt_ps, dt_dve, dt_act, dtr_ps, dtr_ev, rt_ps, rt_hi, rtm_hi = (
            sem(n) for n in "wd_in wd_hi_ready wd_lo_ready dt_ps dt_dve dt_act dtr_ps dtr_ev rt_ps rt_hi rtm_hi".split())
        rt_ready, cum_ps, ex_ready, wT_ready = (
            sem(n) for n in "rt_ready cum_ps ex_ready wT_ready".split())
        tg_ready, v_ready, v_out, pad_zero, pad_ready, cv_ready = (
            sem(n) for n in "tg_ready v_ready v_out pad_zero pad_ready cv_ready".split())
        conv_tap, bc_ready, z_ready, zcopied, small_ready, xt_ps, bt_ps, sc_ps, xt_ready, bt_ready, sc_ready, xw_ready = (
            sem(n) for n in "conv_tap bc_ready z_ready zcopied small_ready xt_ps bt_ps sc_ps xt_ready bt_ready sc_ready xw_ready".split())
        st_ps, st_ready, yoff_ps, yoff_ready, seg_ps, e_ready, t_ready, m_ready, y_ps, y_ready, yt_ps, gate_mid, gated, xd_ready = (
            sem(n) for n in "st_ps st_ready yoff_ps yoff_ready seg_ps e_ready t_ready m_ready y_ps y_ready yt_ps gate_mid gated xd_ready".split())
        gsq, gsq_sum, gst_ps, gln, gr_ready, y2_ready, y_out = (
            sem(n) for n in "gsq gsq_sum gst_ps gln gr_ready y2_ready y_out".split())
        vp_in, cw_ready, unit_tap_done, unit_done, c_out = (
            sem(n) for n in "vp_in cw_ready unit_tap_done unit_done c_out".split())
        yhi_ready, y_split, gate_ready, mix_b = (
            sem(n) for n in "yhi_ready y_split gate_ready mix_b".split())
        cv_in, cv_sum, mu_ps, mu_ready, d_ready, lsq, lsum, lst_ps, lln, lr_ready, n_ready, ns_ready = (
            sem(n) for n in "cv_in cv_sum mu_ps mu_ready d_ready lsq lsum lst_ps lln lr_ready n_ready ns_ready".split())
        chi_ready, c_split, ya_mid, mix_ready, mhi_ready, m_split = (
            sem(n) for n in "chi_ready c_split ya_mid mix_ready mhi_ready m_split".split())
        fin_ready, out_ps, out_ready, out_done = (
            sem(n) for n in "fin_ready out_ps out_ready out_done".split())

        block = ctx.enter_context(nc.Block())
        XL = 2 * KD * len(PARTS) + KD
        X_WO = KD * len(PARTS)
        TAP_SLICES = [(0, 8), (8, 14), (14, 18), (18, 23), (23, 27), (27, 29), (29, DWK), (DWK, DWK)]
        f32 = lambda ap: ap.bitcast(F32)
        chunk = lambda c: slice(c * P, (c + 1) * P)

        def stage_rows(row, n, block):
            return stage[row:row + n, :, :].rearrange("r (l b) p -> r l b p", b=5)[:, :, block, :]

        def gain(L, f, k):
            if f:
                return prm[:, P_FFN2 + k:P_FFN2 + k + 1]
            return prm2[:, bass.ds(L, 1), P_FFN1 + k:P_FFN1 + k + 1].rearrange("p l c -> p (l c)")

        @block.sync
        def _(sp):
            def load(s, slot, src):
                sp.wait_ge(lo_ready, s + 1)
                k = src.shape[1]
                dst = wraw[:, slot, 0:k * P].rearrange("p (k m) -> p k m", m=P)
                sp.dma_start(dst, src).then_inc(raw_in[slot], 16)

            for r in range(2):
                src = (x_prompt, x_sample)[r].rearrange("b (c p) d -> p (b c) d", p=P)
                sp.dma_start(x_tm[:, r * CPR:(r + 1) * CPR, :], src).then_inc(x_in, 16)

            def ffn(L, f, base):
                s = L * NSLAB + base
                for p0, n in PARTS:
                    with sp.Fori(0, n // 2) as i:
                        for q in range(4):
                            col = i * (2 * P) + ((p0 + q // 2) * P + (q % 2) * FF)
                            load(s + i * 4 + q, q, W_UP[f][:, bass.ds(L * KD, KD), bass.ds(col, P)])
                    s = s + 2 * n
                    with sp.Fori(0, KD // 4) as i:
                        for q in range(4):
                            load(s + i * 4 + q, q,
                                 W_DOWN[f][:, bass.ds(L * FT + p0, n), bass.ds(i * (4 * P) + q * P, P)])
                    s = s + KD

            def columns(L, base, w, col):
                with sp.Fori(0, KD // 4) as i:
                    for q in range(4):
                        load(L * NSLAB + base + i * 4 + q, q,
                             w[:, bass.ds(L * KD, 8), bass.ds(i * (4 * P) + (q * P + col), P)])

            with sp.Fori(0, DEPTH) as L:
                ffn(L, 0, 0)
                with sp.Fori(0, NG) as g:
                    s = L * NSLAB + g * 8 + S_GROUP
                    cols = [g * P + C_GATE, g * P + C_A, g * P + C_B, g * P + C_C,
                            g * (2 * P) + C_X, g * (2 * P) + (C_X + P), g * (2 * P) + C_Z, g * (2 * P) + (C_Z + P)]
                    for t in range(8):
                        load(s + t, t % RING, W_IN[:, bass.ds(L * KD, 8), bass.ds(cols[t], P)])
                columns(L, S_GB, W_IN, C_GB)
                columns(L, S_GA, W_IN, C_GA)
                with sp.Fori(0, KD // 2) as i:
                    for q in range(4):
                        load(L * NSLAB + S_SSDO + i * 4 + q, q,
                             W_SSD[:, bass.ds(L * XT_ + 8 * (q % 2), 8), bass.ds(i * (2 * P) + (q // 2) * P, P)])
                columns(L, S_CONF, W_CONF, 0)
                columns(L, S_WO, W_O, 0)
                ffn(L, 1, S_FFN2)
            for q in range(AHEAD):
                load(DEPTH * NSLAB + q, q, W_UP[0][:, 0:KD, q * P:(q + 1) * P])
            for c in range(NC):
                sp.wait_ge(out_ready, NC + c + 1)
                dst = io["out_0"] if c < CPR else io["out_1"]
                sp.dma_start(dst[0, (c % CPR) * P:(c % CPR + 1) * P, :], o_tm[:, c, :]).then_inc(out_done, 16)
            sp.wait_ge(out_done, 16 * NC)

        @block.gpsimd
        def _(pool):
            g_ = nc.gpsimd
            for free, n in ((lo_ready, RING), (slab_done, RING), (sq_added, 1), (ab_free, 2), (pad_ready, 2), (cv_ready, 2), (z_ready, 2),
                            (conv_tap, 1), (xt_ps, 1), (xw_ready, 1), (yoff_ps, 1), (yoff_ready, 1), (sc_ps, 1),
                            (seg_ps, 1), (e_ready, 1), (m_ready, 1), (y_ps, 1), (y_ready, 1), (gated, 1), (xd_ready, 1),
                            (gst_ps, 1), (y2_ready, 1), (unit_tap_done, 1), (unit_done, 1), (y_split, 4), (ya_mid, 2)):
                pool.sem_inc(free, n)
            g_.memset(ident[:, :], 0.0).then_inc(const_made, 1)
            g_.memset(ones[:, :], 1.0).then_inc(const_made, 1)
            g_.memset(ul[:, :, :], 1.0).then_inc(const_made, 1)
            g_.memset(selr[:, :, :], 0.0).then_inc(const_made, 1)
            g_.memset(eps_t[:, :], EPS).then_inc(const_made, 1)
            pool.wait_ge(const_made, 5)
            g_.affine_select(out=ident[:, :], in_=ident[:, :], compare_op=ALU.not_equal, fill=1.0, base=0,
                             pattern=[[-1, P]], channel_multiplier=1).then_inc(const_fix, 1)
            g_.affine_select(out=ul[:, 0, :], in_=ul[:, 0, :], compare_op=ALU.is_ge, fill=0.0, base=0,
                             pattern=[[1, P]], channel_multiplier=-1).then_inc(const_fix, 1)
            g_.affine_select(out=ul[:, 1, :], in_=ul[:, 1, :], compare_op=ALU.is_ge, fill=0.0, base=0,
                             pattern=[[-1, P]], channel_multiplier=1).then_inc(const_fix, 1)
            n = 3
            for sign in range(2):
                for half in range(2):
                    pool.wait_ge(const_fix, n)
                    pool.sem_inc(pool_passed, 1)
                    g_.affine_select(out=selr[:, sign, :], in_=selr[:, sign, :], compare_op=ALU.not_equal,
                                     fill=1.0 - 2 * sign, base=-half * 2 * NH, pattern=[[-1, 2 * NH]],
                                     channel_multiplier=1).then_inc(const_fix, 1)
                    n += 1
            pool.wait_ge(const_fix, 7)
            g_.tensor_scalar(neverf[:, :, :], ul[:, :, :], -1.0, BIG, ALU.add, ALU.mult).then_inc(const_fix, 1)
            for row, name, free in ((0, "ffn1_norm", v_out), (KD, "mix_norm", y_out), (2 * KD, "ffn2_norm", c_out)):
                g_.dma_start(stage_rows(row, KD, 0), io[name].rearrange("l (t p) -> t l p", p=P)).then_inc(free, 16)

            def group(L, g, slabs, ssd, norm):
                G = L * NG + g
                H = G - 1
                if ssd:
                    pool.wait_ge(seg_ps, H * NC + 1)
                    pool.wait_ge(yoff_ready, H * NB + 1)
                    pool.wait_ge(xw_ready, H + 1)
                    pool.wait_ge(ex_ready, L + 1)
                    pool.wait_ge(wT_ready, L + 1)
                    pool.sem_inc(pool_passed, 1)
                    h0 = g * HPG - HPG
                    src = selr[:, :, :].rearrange("p s (d h) -> p s d h", d=2)[:, :, :, bass.ds(h0, HPG)]
                    g_.tensor_copy(selg[:, :, :, :], src).then_inc(small_ready, 1)
                    for c in range(2):
                        src = wT[:, c:NC:2, bass.ds(h0 + c * NH, HPG)]
                        g_.tensor_copy(wg[:, c:NC:2, :], src).then_inc(small_ready, 1)
                    src = exT[:, :, :].rearrange("p (b c) x -> p b (c x)", b=2)[:, :, NH:3 * NH]
                    src = src.rearrange("p b (c h) -> p b c h", c=2)[:, :, :, bass.ds(h0, HPG)]
                    g_.tensor_copy(exg[:, :, :].rearrange("p (b c) h -> p b c h", b=2), src).then_inc(small_ready, 1)
                    pool.wait_ge(v_out, G * 16 + 16)
                    pool.wait_ge(pad_zero, L * 2 + 2)
                    pool.wait_ge(unit_done, H + 1)
                    pool.sem_inc(pool_passed, 1)
                    pool.dma_start(vp[:, :, HALO:HALO + SEQ],
                                   v_dram[:, bass.ds(g - 1, 1)].rearrange("r o p t -> p (r o) t")).then_inc(vp_in, 16)
                if slabs:
                    pool.wait_ge(v_ready, G + 1)
                    pool.sem_inc(pool_passed, 1)
                    pool.dma_start(v_dram[:, bass.ds(g, 1)].rearrange("r o p t -> p (r o) t"),
                                   tg[:, :].rearrange("p (r t) -> p r t", r=2)).then_inc(v_out, 16)
                if norm:
                    pool.wait_ge(y2_ready, G * 2 - 1)
                    pool.sem_inc(pool_passed, 1)
                    pool.dma_start(y_dram[bass.ds(g * 2 - 4, 2)].rearrange("k p t -> p k t"),
                                   yz[:, :, :]).then_inc(y_out, 16)
                if ssd:
                    pool.wait_ge(unit_done, H + 2)
                    pool.sem_inc(pool_passed, 1)
                    pool.dma_start(c_dram[:, bass.ds(g - 1, 1)].rearrange("r o p t -> p (r o) t"),
                                   cacc[:, 0, :].rearrange("p (r t) -> p r t", r=2)).then_inc(c_out, 16)

            with pool.Fori(0, DEPTH) as L:
                pool.wait_ge(prm2_ready, 2 * DEPTH + 4)
                pool.wait_ge(x_done, L * XL + KD)
                pool.sem_inc(pool_passed, 1)
                pool.dma_start(wd_raw[:, :, :], W_IN[:, bass.ds(L * KD, KD), C_DT:C_DT + P]).then_inc(wd_in, 16)
                group(L, 0, True, False, False)
                group(L, 1, True, True, False)
                with pool.Fori(2, NG) as g:
                    group(L, g, True, True, True)
                group(L, NG, False, True, True)
                group(L, NG + 1, False, False, True)
                pool.wait_ge(gated, (L * NG + NG) * NB + 1)
                pool.wait_ge(y_out, (L * NG + NG) * 16)
                for k in range(XT_):
                    if k == XT_ - 2:
                        pool.wait_ge(y_out, (L * NG + NG) * 16 + 16)
                    pool.wait_ge(y_split, L * XT_ + k + 1)
                    pool.sem_inc(pool_passed, 1)
                    pool.dma_start(yraw[:, k % 4, :], y_dram[k]).then_inc(yr_in[k % 4], 16)
                pool.wait_ge(c_out, (L * NG + NG) * 16 + 16)
                pool.wait_ge(y_split, L * XT_ + XT_ + 4)
                pool.sem_inc(pool_passed, 1)
                for r in range(2):
                    pool.dma_start(cv[:, :, r * SEQ:(r + 1) * SEQ],
                                   c_dram[r].rearrange("k p t -> p k t")).then_inc(cv_in, 16)

        @block.scalar
        def _(act):
            a_ = nc.scalar

            def split(s4, q):
                t = q + AHEAD
                act.wait_ge(raw_in[t % RING], s4 * 16 + 16 * (t // RING + 1))
                act.wait_ge(slab_done, s4 * 4 + (t + 1))
                a_.activation(whi[:, t % RING, :], wraw[:, t % RING, :], ACT.Copy).then_inc(hi_ready, 1)

            def square(N, x_base, k):
                act.wait_ge(x_done, x_base + k + 1)
                act.wait_ge(sq_added, N * (KD - 1) + (0 if k < 2 else max(k - 2, 1)) + 1)
                a_.activation(sq[:, k % 2, :], xf[:, k, :], ACT.Square).then_inc(sq_ready, 1)

            names = ["ffn1_norm", "mix_norm", "ffn2_norm", None, "conf_ln_g", "conf_ln_b", "conf_dw_b",
                     "ssd_norm", "ssd_conv_b", "gate_bias"]
            row = 0
            for name in names:
                n = (io[name][0] if name else io["final_norm"]).shape[0] // P
                if name is None:
                    for l in range(DEPTH):
                        a_.dma_start(stage[row:row + n, 5 * l, :], io["final_norm"].rearrange("(t p) -> t p", p=P)).then_inc(consts_in, 16)
                elif row >= 3 * KD:
                    a_.dma_start(stage_rows(row, n, 0), io[name].rearrange("l (t p) -> t l p", p=P)).then_inc(consts_in, 16)
                row += n
            for b, name in ((1, "conf_dw_w"), (3, "ssd_conv_w")):
                src = io[name].rearrange("l k (t p) -> (k t) l p", p=P)
                a_.dma_start(stage_rows(0, P, b), src[0:P]).then_inc(consts_in, 16)
                a_.dma_start(stage_rows(0, src.shape[0] - P, b + 1), src[P:]).then_inc(consts_in, 16)
            a_.dma_start(dall[:, :, :], io["ssd_D"].unsqueeze(0).broadcast_to([P, DEPTH, NH])).then_inc(consts_in, 16)
            for l in range(DEPTH):
                for j, name in enumerate(("ssd_dt_bias", "ssd_A_log")):
                    a_.dma_start(dtbA[:, j, l:l + 1],
                                 io[name][l].rearrange("d (h o) -> (d h) o", o=1)).then_inc(consts_in, 16)
            act.wait_ge(const_made, 5)
            for k in range(KD - 1):
                square(0, 0, k)
            for l in range(DEPTH):
                act.wait_ge(prm_ps, 2 * l + 1)
                a_.activation(prm2[:, l, 0:PB], bank[2 + 2 * l][:, 0:PB], ACT.Copy).then_inc(prm2_ready, 1)
                act.wait_ge(prm_ps, 2 * l + 2)
                a_.activation(prm2[:, l, PB:NPRM], bank[3 + 2 * l][:, 0:NPRM - PB], ACT.Copy).then_inc(prm2_ready, 1)
            act.wait_ge(const_fix, 8)
            a_.activation(identr[:, :], ident[:, :], ACT.Copy).then_inc(prm2_ready, 1)
            a_.activation(never[:, :, :], neverf[:, :, :], ACT.Copy).then_inc(prm2_ready, 1)
            for half in range(2):
                rows = slice(half * HEAD, (half + 1) * HEAD)
                a_.activation(dskip[rows, :].rearrange("p (l t) -> p l t", l=DEPTH), dall[rows, :, half:NH:2], ACT.Copy).then_inc(prm2_ready, 1)
            a_.activation(negA[:, :], dtbA[:, 1, :], ACT.Exp).then_inc(negA_exp, 1)
            for t in range(AHEAD):
                act.wait_ge(raw_in[t], 16)
                a_.activation(whi[:, t, :], wraw[:, t, :], ACT.Copy).then_inc(hi_ready, 1)
            act.wait_ge(prm2_ready, 2 * DEPTH + 4)

            def split_and_square(s4, N, x_base):
                for k in range(KD):
                    split(s4 + k // 4, k % 4)
                    if k:
                        square(N, x_base, k - 1)

            def norm_root(N):
                act.wait_ge(stat_mm, N + 1)
                a_.activation(rbc[:, :], bank[6][:, :], ACT.Ln, scale=1.0 / DM, bias=eps_t[:, 0:1]).then_inc(lnr, 1)
                act.wait_ge(lnr, N + 1)
                a_.activation(rbc[:, :], rbc[:, :], ACT.Exp, scale=-0.5).then_inc(r_ready, 1)

            def ffn(L, f, base):
                N = L * 3 + 2 * f
                xb = L * XL + (KD - KD if f == 0 else X_WO + KD)
                if f:
                    act.wait_ge(prm_ready, L * 2 + 2)
                for k in range(KD):
                    act.wait_ge(x_done, xb + k + 1)
                    if k == 0:
                        act.wait_ge(slab_done, L * NSLAB + base + RING)
                    a_.activation(uhi[:, k, :], xf[:, k, :], ACT.Copy, scale=gain(L, f, k)).then_inc(nhi_ready, 1)
                square(N, xb, KD - 1)
                norm_root(N)
                s4 = L * (NSLAB // 4) + base // 4
                for part, (p0, n) in enumerate(PARTS):
                    with act.Fori(0, n // 2) as i:
                        for j in range(2):
                            PI = L * (2 * FT) + (f * FT + p0 + j) + i * 2
                            split(s4 + i, 2 * j)
                            act.wait_ge(fa_ready, PI + 1)
                            a_.activation(fa[:, j, :], fa[:, j, :], ACT.Silu).then_inc(silu_ready, 1)
                            split(s4 + i, 2 * j + 1)
                            act.wait_ge(h_ready, PI + 1)
                            a_.activation(hhi[:, bass.ds(i * 2 + j, 1), :], fb[:, j:j + 1, :], ACT.Copy).then_inc(hhi_ready, 1)
                    s4 = s4 + n // 2
                    if part == len(PARTS) - 1:
                        split_and_square(s4, N + 1, L * XL + (X_WO if f == 0 else XL))
                        break
                    with act.Fori(0, KD // 4) as i:
                        for q in range(4):
                            split(s4 + i, q)
                    s4 = s4 + KD // 4

            def dt_steps(L, t):
                if t == 0:
                    act.wait_ge(dt_dve, L * ND + 1)
                    a_.activation(de[:, :], dx[:, :], ACT.Abs).then_inc(dt_act, 1)
                    act.wait_ge(dt_act, L * NA + 1)
                    a_.activation(de[:, :], de[:, :], ACT.Exp, scale=-1.0).then_inc(dt_act, 1)
                    act.wait_ge(dt_dve, L * ND + 2)
                    a_.activation(dl[:, :], du[:, :], ACT.Ln).then_inc(dt_act, 1)
                if t == 1:
                    act.wait_ge(dt_dve, L * ND + 10)
                    a_.activation(dl[:, :], dl[:, :], ACT.Ln).then_inc(dt_act, 1)
                if t == 2:
                    act.wait_ge(dtr_ps, L + 1)
                    a_.activation(dtT[:, :, :], bank[6][:, 0:2 * T // 4].rearrange("p (c x) -> p c x", c=NC), ACT.Copy).then_inc(dtr_ev, 1)
                    a_.activation(aT[:, :, :], bank[6][:, 2 * T // 4:].rearrange("p (c x) -> p c x", c=NC), ACT.Copy).then_inc(dtr_ev, 1)
                if t == 3:
                    act.wait_ge(rt_ps, L + 1)
                    for b in range(2):
                        for d in range(2):
                            rows = slice(d * NH, (d + 1) * NH)
                            src = bank[2 + b][rows, :].rearrange("p (c d i) -> p c d i", c=2, d=2)[:, :, d, :]
                            a_.activation(rt[rows, 2 * b:2 * b + 2, :], src, ACT.Copy).then_inc(rt_hi, 1)
                    act.wait_ge(cum_ps, L + 1)
                    a_.activation(cumS[:, :, :], bank[4][:, 0:256].rearrange("p (c x) -> p c x", c=NC), ACT.Copy).then_inc(dt_act, 1)
                if t == 4:
                    act.wait_ge(dt_act, L * NA + 5)
                    a_.activation(exT[:, :, :], cumS[:, :, :], ACT.Exp).then_inc(ex_ready, 1)
                    act.wait_ge(dt_dve, L * ND + ND)
                    a_.activation(ddS[:, :, :], ddS[:, :, :], ACT.Exp).then_inc(dt_act, 1)
                    a_.activation(rtm[0:2 * NH, :, :], dc[:, :].rearrange("p (c i) -> p c i", c=NC), ACT.Copy).then_inc(rtm_hi, 1)

            def group(L, g, slabs, ssd, norm, gate=None):
                G = L * NG + g
                H, n = G - 1, G - 2
                s4 = L * (NSLAB // 4) + g * 2 + S_GROUP // 4

                def step(t):
                    act.wait_ge(slab_done, (s4 + t // 4) * 4 + (t % 4 + 1) + RING)

                def conv_silu(GG, j):
                    act.wait_ge(cv_ready, GG * 4 + j + 3)
                    a_.activation(bc[:, j, :], bc[:, j, :], ACT.Silu).then_inc(bc_ready, 1)

                def exp_seg(c):
                    act.wait_ge(seg_ps, H * NC + c + 2)
                    for d in range(2):
                        a_.activation(E[:, c, d, :], bank[2 + 4 * (c % 2) + d][:, :], ACT.Exp).then_inc(e_ready, 1)

                for t in range(8):
                    if t == 0:
                        if norm:
                            act.wait_ge(gated, n * NB + NB + 1)
                            act.wait_ge(gst_ps, n + 1)
                            for j in range(2):
                                a_.activation(sq[:, j, :], yz[:, j, :], ACT.Square).then_inc(gsq, 1)
                        if ssd:
                            conv_silu(H, 2)
                            conv_silu(H, 3)
                            act.wait_ge(z_ready, H * 2 + 4)
                            act.wait_ge(gated, H * NB + 1)
                            for j in range(2):
                                a_.activation(zcur[:, j, :], znew[:, j, :], ACT.Copy).then_inc(zcopied, 1)
                    if slabs or gate:
                        split(s4 + t // 4, t % 4)
                    if t == 0 and ssd:
                        act.wait_ge(y_ps, H * NB + 1)
                    if gate:
                        if t != 2 or not ssd:
                            step(t)
                            gate(t)
                    if slabs and t == 0:
                        step(0)
                        act.wait_ge(v_out, G * 16 + 16)
                        a_.activation(tg[:, :], bank[0][:, :], ACT.Tanh, scale=0.5).then_inc(tg_ready, 1)
                    if t == 0 and ssd:
                        for b in range(2):
                            act.wait_ge(xt_ps, H * 2 + b + 2)
                            a_.activation(xT[:, 2 * b:2 * b + 2, :], bank[2 + b][:, :].rearrange("p (c f) -> p c f", c=2),
                                          ACT.Copy).then_inc(xt_ready, 1)
                        act.wait_ge(bt_ps, H + 1)
                        a_.activation(bT[:, :, :], bank[4][:, :].rearrange("p (c f) -> p c f", c=NC), ACT.Copy).then_inc(bt_ready, 1)
                        act.wait_ge(sc_ps, H + 2)
                        act.wait_ge(m_ready, H * NC + 1)
                        a_.activation(SC[:, :, :], bank[5][:, :].rearrange("p (c f) -> p c f", c=NC), ACT.Copy).then_inc(sc_ready, 1)
                    if t == 1 and norm:
                        act.wait_ge(gst_ps, n + 2)
                        act.wait_ge(y2_ready, n * 2 + 1)
                        a_.activation(rg[:, :], bank[4][:, :], ACT.Ln, scale=1.0 / GF, bias=eps_t[:, 0:1]).then_inc(gln, 1)
                        act.wait_ge(gln, n + 1)
                        a_.activation(rg[:, :], rg[:, :], ACT.Exp, scale=-0.5).then_inc(gr_ready, 1)
                    if slabs and 2 <= t < 6:
                        step(t)
                        act.wait_ge(pad_zero, L * 2 + 2)
                        act.wait_ge(cv_ready, G * 4 + t - 1)
                        a_.activation(xpad[:, t % 2, :, 2:2 + SEQ], bank[t % 2][:, :].rearrange("p (r t) -> p r t", r=2),
                                      ACT.Copy).then_inc(pad_ready, 1)
                    if ssd and t in (1, 2):
                        exp_seg(2 * t - 2)
                        exp_seg(2 * t - 1)
                    if gate and t == 2 and ssd:
                        step(2)
                        gate(2)
                    if slabs and t in (6, 7):
                        step(t)
                        if t == 6 and ssd:
                            act.wait_ge(zcopied, G * 2)
                        a_.activation(znew[:, t - 6, :], bank[t % 2][:, :], ACT.Silu).then_inc(z_ready, 1)
                    if slabs and t >= 6:
                        conv_silu(G, t - 6)
                    if ssd and t == 3:
                        for b in range(2):
                            act.wait_ge(st_ps, H * 2 + b + 1)
                            a_.activation(xw[:, 2 * b:2 * b + 2, :], bank[6 + b][:, :].rearrange("p (c f) -> p c f", c=2),
                                          ACT.Copy).then_inc(st_ready, 1)
                    if ssd and t == 4:
                        act.wait_ge(y_out, H * 16 + 16)
                        for j in range(2):
                            a_.activation(yz[:, j, :], bc[:, 2 + j, :], ACT.Copy,
                                          scale=dskip[:, bass.ds(L * XT_ + g * 2 + (j - 2), 1)]).then_inc(xd_ready, 1)
                    if slabs and not ssd:
                        dt_steps(L, t)

            def y_hi(L, k):
                act.wait_ge(yr_in[k % 4], L * (XT_ // 4 * 16) + 16 * (k // 4 + 1))
                dst = hhi[:, k, :] if k < KD else phi[:, k - KD, :]
                a_.activation(dst, yraw[:, k % 4, :], ACT.Copy).then_inc(yhi_ready, 1)

            with act.Fori(0, DEPTH) as L:
                ffn(L, 0, 0)
                act.wait_ge(wd_in, L * 16 + 16)
                a_.activation(wd_hi[:, :, :], wd_raw[:, :, :], ACT.Copy).then_inc(wd_hi_ready, 1)
                N = L * 3 + 1
                square(N, L * XL + X_WO, KD - 1)
                norm_root(N)
                for k in range(KD):
                    act.wait_ge(nt_ready, L * KD + k + 1)
                    a_.activation(uhi[:, k, :], sq[:, k % 2, :], ACT.Copy).then_inc(nhi_ready, 1)
                group(L, 0, True, False, False)
                group(L, 1, True, True, False)
                with act.Fori(2, NG) as g:
                    group(L, g, True, True, True)

                def gate_b(t):
                    if t == 0:
                        act.wait_ge(dt_act, L * NA + NA)
                    a_.activation(mix[:, t, :], bank[t % 2][:, :], ACT.Tanh, scale=0.5,
                                  bias=hbias[:, KD + t:KD + t + 1]).then_inc(gate_ready, 1)

                def gate_a(t):
                    a_.activation(ga[:, t, :], bank[t % 2][:, :], ACT.Tanh, scale=0.5,
                                  bias=hbias[:, t:t + 1]).then_inc(gate_ready, 1)
                    if t >= 4:
                        y_hi(L, t - 4)

                group(L, NG, False, True, True, gate=gate_b)
                group(L, NG + 1, False, False, True, gate=gate_a)
                for k in range(4, XT_):
                    if k == KD:
                        act.wait_ge(slab_done, L * NSLAB + S_SSDO + RING)
                    y_hi(L, k)
                s4 = L * (NSLAB // 4)
                for i in range(KD // 2):
                    for q in range(4):
                        split(s4 + S_SSDO // 4 + i, q)
                    if i == 1:
                        act.wait_ge(mu_ps, L + 1)
                        a_.activation(mu[:, :], bank[6][:, :], ACT.Copy, scale=1.0 / DM).then_inc(mu_ready, 1)
                    if i == 1:
                        for k in range(KD):
                            act.wait_ge(d_ready, L * KD + k + 1)
                            if k >= 2:
                                act.wait_ge(lsum, L * (KD - 1) + max(k - 2, 1))
                            a_.activation(sq[:, k % 2, :], cv[:, k, :], ACT.Square).then_inc(lsq, 1)
                    if i == 2:
                        act.wait_ge(lst_ps, L + 1)
                        a_.activation(rbc[:, :], bank[7][:, :], ACT.Ln, scale=1.0 / DM, bias=eps_t[:, 0:1]).then_inc(lln, 1)
                        act.wait_ge(lln, L + 1)
                        a_.activation(rbc[:, :], rbc[:, :], ACT.Exp, scale=-0.5).then_inc(lr_ready, 1)
                        for k in range(KD):
                            act.wait_ge(n_ready, L * KD + k + 1)
                            a_.activation(cv[:, k, :], cv[:, k, :], ACT.Silu, scale=prm[:, P_LNG + k:P_LNG + k + 1],
                                          bias=prm[:, P_LNB + k:P_LNB + k + 1]).then_inc(ns_ready, 1)
                act.wait_ge(slab_done, L * NSLAB + S_CONF - 1 + RING)
                for k in range(KD):
                    act.wait_ge(ns_ready, L * KD + k + 1)
                    a_.activation(hhi[:, k, :], cv[:, k, :], ACT.Copy).then_inc(chi_ready, 1)
                with act.Fori(0, KD // 4) as i:
                    for q in range(4):
                        split(s4 + S_CONF // 4 + i, q)
                        act.wait_ge(mix_ready, L * KD + i * 4 + q + 1)
                        m = bass.ds(i * 4 + q, 1)
                        a_.activation(uhi[:, m, :], mix[:, m, :], ACT.Copy).then_inc(mhi_ready, 1)
                split_and_square(s4 + S_WO // 4, L * 3 + 2, L * XL + X_WO + KD)
                ffn(L, 1, S_FFN2)
            square(3 * DEPTH, DEPTH * XL, KD - 1)
            norm_root(3 * DEPTH)
            for half in range(2):
                for c in range(NC):
                    act.wait_ge(out_ps, NC * half + c + 1)
                    a_.activation(o_tm[:, c, half * 512:(half + 1) * 512], bank[c][:, :], ACT.Copy).then_inc(out_ready, 1)

        @block.vector
        def _(dve):
            v_ = nc.vector

            def split(s4, q):
                t = q + AHEAD
                dve.wait_ge(hi_ready, s4 * 4 + (t + 1))
                v_.tensor_tensor(wlo[:, t % RING, :], wraw[:, t % RING, :], f32(whi[:, t % RING, :]), ALU.subtract).then_inc(lo_ready, 1)

            def add_square(N, k):
                dve.wait_ge(sq_ready, N * KD + k + 1)
                if k == 1:
                    if not isinstance(N, int) or N > 0:
                        dve.wait_ge(stat_mm, N)
                    v_.tensor_tensor(acc[:, :], sq[:, 0, :], sq[:, 1, :], ALU.add).then_inc(sq_added, 1)
                elif k > 1:
                    dve.wait_ge(sq_added, N * (KD - 1) + k)
                    v_.tensor_tensor(acc[:, :], acc[:, :], sq[:, k % 2, :], ALU.add).then_inc(sq_added, 1)

            for m in range(KD):
                dve.wait_ge(x_ps, m + 1)
                v_.tensor_copy(xf[:, m, :], bank[m % 2][:, :]).then_inc(x_done, 1)
            for k in range(1, KD - 1):
                add_square(0, k)
            dve.wait_ge(negA_exp, 1)
            v_.tensor_scalar(negA[:, :], negA[:, :], -1.0, None, ALU.mult).then_inc(negA_ready, 1)
            dve.wait_ge(negA_ready, 1)
            for t in range(AHEAD):
                dve.wait_ge(hi_ready, t + 1)
                v_.tensor_tensor(wlo[:, t, :], wraw[:, t, :], f32(whi[:, t, :]), ALU.subtract).then_inc(lo_ready, 1)
            dve.wait_ge(prm2_ready, 2 * DEPTH + 4)

            def update_x(s4, b0, x_base, N):
                for k in range(KD):
                    split(s4 + k // 4, k % 4)
                    dve.wait_ge(slab_done, s4 * 4 + (k + 1) + RING)
                    dve.wait_ge(x_done, x_base + k + 1)
                    v_.scalar_tensor_tensor(out=xf[:, k, :], in0=bank[b0 + k % 2][:, :], scalar=0.5,
                                            in1=xf[:, k, :], op0=ALU.mult, op1=ALU.add).then_inc(x_done, 1)
                    if k:
                        add_square(N, k - 1)

            def norm_low(L, f, N):
                for k in range(KD):
                    dve.wait_ge(nhi_ready, N * KD + k + 1)
                    v_.scalar_tensor_tensor(out=ulo[:, k, :], in0=xf[:, k, :], scalar=gain(L, f, k),
                                            in1=f32(uhi[:, k, :]), op0=ALU.mult, op1=ALU.subtract).then_inc(u_ready, 1)

            def ffn(L, f, base):
                N = L * 3 + 2 * f
                xb = L * XL + (KD if f == 0 else X_WO + 2 * KD)
                norm_low(L, f, N)
                add_square(N, KD - 1)
                if f == 0:
                    src = prm2[:, bass.ds(L, 1), :]
                    v_.tensor_copy(prm[:, :].unsqueeze(1), src).then_inc(prm_ready, 1)
                    v_.tensor_scalar(hbias[:, :].unsqueeze(1), src[:, :, P_GBIAS:P_GBIAS + 2 * KD], 0.5, None, ALU.mult).then_inc(prm_ready, 1)
                    dve.wait_ge(prm_ready, L * 2 + 2)
                dve.wait_ge(r_ready, N + 1)
                dve.sem_inc(dve_passed, 1)
                s4 = L * (NSLAB // 4) + base // 4
                for part, (p0, n) in enumerate(PARTS):
                    with dve.Fori(0, n // 2) as i:
                        for j in range(2):
                            PI = L * (2 * FT) + (f * FT + p0 + j) + i * 2
                            split(s4 + i, 2 * j)
                            dve.wait_ge(slab_done, (s4 + i) * 4 + 2 * j + 1 + RING)
                            v_.tensor_tensor(fa[:, j, :], bank[2 * j][:, :], rbc[:, :], ALU.mult).then_inc(fa_ready, 1)
                            split(s4 + i, 2 * j + 1)
                            dve.wait_ge(slab_done, (s4 + i) * 4 + 2 * j + 2 + RING)
                            v_.tensor_tensor(fb[:, j, :], bank[2 * j + 1][:, :], rbc[:, :], ALU.mult).then_inc(ab_free, 1)
                            dve.wait_ge(ab_free, PI + 3)
                            dve.wait_ge(silu_ready, PI + 1)
                            v_.tensor_tensor(fb[:, j, :], fa[:, j, :], fb[:, j, :], ALU.mult).then_inc(h_ready, 1)
                            dve.wait_ge(hhi_ready, PI + 1)
                            m = bass.ds(i * 2 + j, 1)
                            v_.tensor_tensor(hlo[:, m, :], fb[:, j:j + 1, :], f32(hhi[:, m, :]), ALU.subtract).then_inc(hlo_ready, 1)
                    s4 = s4 + n // 2
                    if part == len(PARTS) - 1:
                        update_x(s4, 4, xb + part * KD - KD, N + 1)
                        break
                    with dve.Fori(0, KD // 4) as i:
                        for q in range(4):
                            split(s4 + i, q)
                            dve.wait_ge(slab_done, (s4 + i) * 4 + q + 1 + RING)
                            dve.wait_ge(x_done, xb + part * KD - KD + i * 4 + q + 1)
                            m = bass.ds(i * 4 + q, 1)
                            v_.scalar_tensor_tensor(out=xf[:, m, :], in0=bank[4 + q % 2][:, :].unsqueeze(1), scalar=0.5,
                                                    in1=xf[:, m, :], op0=ALU.mult, op1=ALU.add).then_inc(x_done, 1)
                    s4 = s4 + KD // 4

            def dt_steps(L, t):
                d0 = L * ND
                if t == 0:
                    dve.wait_ge(dt_ps, L + 1)
                    v_.tensor_scalar(dx[:, :], bank[5][0:2 * NH, :], dtbA[:, 0, bass.ds(L, 1)], None, ALU.add).then_inc(dt_dve, 1)
                    dve.wait_ge(dt_act, L * NA + 2)
                    v_.tensor_scalar(du[:, :], de[:, :], 1.0, None, ALU.add).then_inc(dt_dve, 1)
                    dve.wait_ge(dt_dve, d0 + 2)
                    v_.tensor_scalar(dc[:, :], du[:, :], -1.0, None, ALU.add).then_inc(dt_dve, 1)
                    dve.wait_ge(dt_dve, d0 + 3)
                    v_.tensor_tensor(dc[:, :], de[:, :], dc[:, :], ALU.subtract).then_inc(dt_dve, 1)
                    dve.wait_ge(dt_dve, d0 + 4)
                    v_.reciprocal(de[:, :], du[:, :]).then_inc(dt_dve, 1)
                    dve.wait_ge(dt_dve, d0 + 5)
                    v_.tensor_tensor(dc[:, :], dc[:, :], de[:, :], ALU.mult).then_inc(dt_dve, 1)
                    v_.tensor_scalar(dx[:, :], dx[:, :], 0.0, None, ALU.max).then_inc(dt_dve, 1)
                    dve.wait_ge(dt_dve, d0 + 7)
                    v_.tensor_tensor(dx[:, :], dx[:, :], dc[:, :], ALU.add).then_inc(dt_dve, 1)
                    dve.wait_ge(dt_dve, d0 + 8)
                    dve.wait_ge(dt_act, L * NA + 3)
                    v_.tensor_tensor(dtf[:, 0, :], dx[:, :], dl[:, :], ALU.add).then_inc(dt_dve, 1)
                    dve.wait_ge(dt_dve, d0 + 9)
                    v_.tensor_scalar(dl[:, :], dtf[:, 0, :], 1e-37, None, ALU.max).then_inc(dt_dve, 1)
                    v_.tensor_scalar(dtf[:, 1, :], dtf[:, 0, :], negA[:, bass.ds(L, 1)], None, ALU.mult).then_inc(dt_dve, 1)
                if t == 3:
                    dve.wait_ge(dt_act, L * NA + 4)
                    dve.wait_ge(rt_ps, L + 1)
                    for b in range(2):
                        for d in range(2):
                            dve.wait_ge(rt_hi, L * 4 + 2 * b + d + 1)
                            rows = slice(d * NH, (d + 1) * NH)
                            low = slice((2 + d) * NH, (3 + d) * NH)
                            src = bank[2 + b][rows, :].rearrange("p (c d i) -> p c d i", c=2, d=2)[:, :, d, :]
                            v_.tensor_tensor(rt[low, 2 * b:2 * b + 2, :], src, f32(rt[rows, 2 * b:2 * b + 2, :]), ALU.subtract).then_inc(rt_ready, 1)
                            tokens = slice(2 * b * P, (2 * b + 2) * P)
                            v_.tensor_tensor(dc[rows, tokens].rearrange("p (c i) -> p c i", c=2), src,
                                             dl[rows, tokens].rearrange("p (c i) -> p c i", c=2), ALU.subtract).then_inc(dt_dve, 1)
                    dve.wait_ge(dt_act, L * NA + 5)
                    v_.tensor_tensor(ddS[:, :, :], bank[4][:, 256:512].rearrange("p (c x) -> p c x", c=NC), cumS[:, :, :], ALU.subtract).then_inc(dt_dve, 1)
                if t == 5:
                    dve.wait_ge(dt_act, L * NA + 6)
                    dve.wait_ge(dtr_ev, L * 2 + 2)
                    v_.tensor_tensor(wT[:, :, :], dtT[:, :, :], ddS[:, :, :], ALU.mult).then_inc(wT_ready, 1)
                    dve.wait_ge(rtm_hi, L + 1)
                    v_.tensor_tensor(rtm[2 * NH:P, :, :], dc[:, :].rearrange("p (c i) -> p c i", c=NC), f32(rtm[0:2 * NH, :, :]),
                                     ALU.subtract).then_inc(rt_ready, 1)

            def group(L, g, slabs, ssd, norm, gate=False):
                G = L * NG + g
                H, n = G - 1, G - 2
                s4 = L * (NSLAB // 4) + g * 2 + S_GROUP // 4
                U, tile = H, g - 1

                def unit_tap(k):
                    src = vp[:, :, k:k + SEQ]
                    dst = cacc[:, k % 2, :].rearrange("p (r t) -> p r t", r=2)
                    if k == 0:
                        dve.wait_ge(unit_tap_done, U * DWK + 1)
                        w = prm[:, P_DW:P_CW].rearrange("p (k t) -> p k t", t=KD)[:, :, bass.ds(tile, 1)]
                        v_.tensor_scalar(cwg[:, :].unsqueeze(2), w, 0.5, None, ALU.mult).then_inc(cw_ready, 1)
                        dve.wait_ge(cw_ready, U + 1)
                        dve.wait_ge(vp_in, U * 16 + 16)
                        dve.wait_ge(c_out, U * 16 + 16)
                        v_.tensor_scalar(dst, src, cwg[:, 0:1], prm[:, bass.ds(tile + P_DWB, 1)],
                                         ALU.mult, ALU.add).then_inc(unit_tap_done, 1)
                    elif k == 1:
                        v_.tensor_scalar(dst, src, cwg[:, 1:2], None, ALU.mult).then_inc(unit_tap_done, 1)
                    else:
                        dve.wait_ge(unit_tap_done, U * DWK + k)
                        v_.scalar_tensor_tensor(out=dst, in0=src, scalar=cwg[:, k:k + 1],
                                                in1=dst, op0=ALU.mult, op1=ALU.add).then_inc(unit_tap_done, 1)

                def conv_tap_of(j, k):
                    col = [g + 2 * KD, g + 3 * KD, g * 2, g * 2 + 1][j]
                    dst = bc[:, j, :].rearrange("p (r t) -> p r t", r=2)
                    src = xpad[:, j % 2, :, k:k + SEQ]
                    w = prm[:, bass.ds(col + (P_CW + k * 4 * KD), 1)]
                    if k == 0:
                        dve.wait_ge(pad_ready, G * 4 + j + 3)
                        if j == 0:
                            dve.wait_ge(sc_ps, G + 1)
                        if j == 1:
                            dve.wait_ge(yoff_ps, G * 2 + 1)
                        if j == 2:
                            dve.wait_ge(xd_ready, G * 2 + 1)
                        ins = v_.tensor_scalar(dst, src, w, prm[:, bass.ds(col + P_CB, 1)], ALU.mult, ALU.add)
                    else:
                        dve.wait_ge(conv_tap, G * 16 + 4 * j + k + 1)
                        ins = v_.scalar_tensor_tensor(out=dst, in0=src, scalar=w, in1=dst, op0=ALU.mult, op1=ALU.add)
                    ins.then_inc(cv_ready if k == TAPS - 1 else conv_tap, 1)

                def decays(b):
                    for c in (2 * b, 2 * b + 1):
                        dve.wait_ge(e_ready, H * 2 * NC + 2 * c + 3)
                        v_.tensor_tensor(E[:, c, 0, :], E[:, c, 0, :], E[:, c, 1, :], ALU.add).then_inc(t_ready, 1)
                    dve.wait_ge(sc_ready, H + 1)
                    for c in (2 * b, 2 * b + 1):
                        dve.wait_ge(t_ready, H * NC + c + 1)
                        e = E[:, c, 0, :].rearrange("p (h i) -> p h i", h=HPG)
                        v_.tensor_tensor(e, e, SC[:, c, :].unsqueeze(1).broadcast_to([P, HPG, P]), ALU.mult).then_inc(m_ready, 1)

                def gating(b):
                    dve.wait_ge(yt_ps, H * NB + b + 1)
                    dve.wait_ge(xd_ready, H * 2 + 3)
                    dve.wait_ge(zcopied, H * 2 + 2)
                    part = yz[:, :, 2 * b * P:(2 * b + 2) * P].rearrange("p j (c i) -> p j c i", c=2)
                    v_.tensor_tensor(part, bank[5][:, :].rearrange("p (c j i) -> p j c i", c=2, j=2), part, ALU.add).then_inc(gate_mid, 1)
                    dve.wait_ge(gate_mid, H * NB + b + 1)
                    v_.tensor_tensor(part, part, zcur[:, :, 2 * b * P:(2 * b + 2) * P].rearrange("p j (c i) -> p j c i", c=2),
                                     ALU.mult).then_inc(gated, 1)

                def add_yoff(b):
                    dve.wait_ge(y_ps, H * NB + b + 2)
                    dve.wait_ge(yoff_ready, H * NB + b + 2)
                    if b:
                        dve.wait_ge(yt_ps, H * NB + 1)
                    v_.tensor_tensor(ytm[:, :, :], bank[4][:, :].rearrange("p (c f) -> p c f", c=2),
                                     yoff[:, 2 * b:2 * b + 2, :], ALU.add).then_inc(y_ready, 1)

                for t in range(8):
                    if t == 1 and norm:
                        dve.wait_ge(gsq, n * 2 + 2)
                        v_.tensor_tensor(sq[:, 0, :], sq[:, 0, :], sq[:, 1, :], ALU.add).then_inc(gsq_sum, 1)
                    if t == 1 and slabs:
                        dve.wait_ge(slab_done, (s4 * 4) + 2 + RING)
                        dve.wait_ge(tg_ready, G + 1)
                        v_.scalar_tensor_tensor(out=tg[:, :], in0=tg[:, :], scalar=1.0, in1=bank[1][:, :],
                                                op0=ALU.add, op1=ALU.mult).then_inc(v_ready, 1)
                    if t == 1 and ssd:
                        dve.wait_ge(xt_ready, H * 2 + 2)
                        dve.wait_ge(small_ready, H * 4 + 4)
                        dve.wait_ge(yoff_ps, H * 2 + 1)
                        v_.tensor_tensor(xw[:, :, :].rearrange("p c (h e) -> p (c h) e", h=HPG),
                                         xT[:, :, :].rearrange("p c (h e) -> p (c h) e", h=HPG),
                                         wg[:, :, :].rearrange("p c h -> p (c h)").unsqueeze(2).broadcast_to([P, NC * HPG, HEAD]),
                                         ALU.mult).then_inc(xw_ready, 1)
                    if ssd and t in (2, 3):
                        decays(t - 2)
                    if t == 2 and norm:
                        dve.wait_ge(gr_ready, n + 1)
                        for j in range(2):
                            v_.scalar_tensor_tensor(out=yz[:, j, :], in0=yz[:, j, :],
                                                    scalar=prm[:, bass.ds(g * 2 + (P_SN - 4 + j), 1)], in1=rg[:, :],
                                                    op0=ALU.mult, op1=ALU.mult).then_inc(y2_ready, 1)
                    if t == 5 and ssd:
                        for b in range(2):
                            dve.wait_ge(yoff_ps, H * 2 + b + 2)
                            v_.tensor_tensor(yoff[:, 2 * b:2 * b + 2, :].rearrange("p c (h e) -> p (c h) e", h=HPG),
                                             bank[6 + b][:, :].rearrange("p (x e) -> p x e", e=HEAD),
                                             exg[:, 2 * b:2 * b + 2, :].rearrange("p c h -> p (c h)").unsqueeze(2).broadcast_to([P, 2 * HPG, HEAD]),
                                             ALU.mult).then_inc(yoff_ready, 1)
                    if ssd and t in (5, 6):
                        add_yoff(t - 5)
                    if ssd and t in (6, 7):
                        gating(t - 6)
                    if slabs and not ssd:
                        dt_steps(L, t)
                    taps = range(*TAP_SLICES[t]) if ssd else ()
                    for k in range(max(len(taps), TAPS)):
                        if slabs and t >= 4 and k < TAPS:
                            conv_tap_of(t - 4, k)
                        if k < len(taps):
                            unit_tap(taps[k])
                    if slabs or gate:
                        split(s4 + t // 4, t % 4)
                    if t == 6 and ssd:
                        dve.wait_ge(unit_tap_done, U * DWK + DWK + 1)
                        v_.tensor_tensor(cacc[:, 0, :], cacc[:, 0, :], cacc[:, 1, :], ALU.add).then_inc(unit_done, 1)

            def y_lo(L, k):
                dve.wait_ge(yhi_ready, L * XT_ + k + 1)
                hi, lo = (hhi, hlo) if k < KD else (phi, plo)
                v_.tensor_tensor(lo[:, k % KD, :], yraw[:, k % 4, :], f32(hi[:, k % KD, :]), ALU.subtract).then_inc(y_split, 1)

            with dve.Fori(0, DEPTH) as L:
                ffn(L, 0, 0)
                dve.wait_ge(wd_hi_ready, L + 1)
                v_.tensor_tensor(wd_lo[:, :, :], wd_raw[:, :, :], f32(wd_hi[:, :, :]), ALU.subtract).then_inc(wd_lo_ready, 1)
                N = L * 3 + 1
                add_square(N, KD - 1)
                dve.wait_ge(r_ready, N + 1)
                for k in range(KD + 1):
                    if k < KD:
                        dve.wait_ge(u_ready, N * KD + k - 1)
                        v_.scalar_tensor_tensor(out=sq[:, k % 2, :], in0=xf[:, k, :], scalar=prm[:, P_MIX + k:P_MIX + k + 1],
                                                in1=rbc[:, :], op0=ALU.mult, op1=ALU.mult).then_inc(nt_ready, 1)
                    if k:
                        dve.wait_ge(nhi_ready, N * KD + k)
                        v_.tensor_tensor(ulo[:, k - 1, :], sq[:, (k - 1) % 2, :], f32(uhi[:, k - 1, :]), ALU.subtract).then_inc(u_ready, 1)
                v_.memset(xpad[:, :, :, :], 0.0).then_inc(pad_zero, 1)
                v_.memset(vp[:, :, :], 0.0).then_inc(pad_zero, 1)
                group(L, 0, True, False, False)
                group(L, 1, True, True, False)
                with dve.Fori(2, NG) as g:
                    group(L, g, True, True, True)
                group(L, NG, False, True, True, gate=True)
                group(L, NG + 1, False, False, True, gate=True)
                for k in range(XT_):
                    y_lo(L, k)
                s4 = L * (NSLAB // 4)
                for i in range(KD // 2):
                    for q in range(4):
                        if i == 1 and q == 1:
                            dve.wait_ge(cv_in, L * 32 + 32)
                            v_.tensor_tensor(acc[:, :], cv[:, 0, :], cv[:, 1, :], ALU.add).then_inc(cv_sum, 1)
                            for k in range(2, KD):
                                dve.wait_ge(cv_sum, L * (KD - 1) + k - 1)
                                v_.tensor_tensor(acc[:, :], acc[:, :], cv[:, k, :], ALU.add).then_inc(cv_sum, 1)
                        if i == 2 and q == 0:
                            dve.wait_ge(mu_ready, L + 1)
                            for k in range(KD):
                                v_.tensor_tensor(cv[:, k, :], cv[:, k, :], mu[:, :], ALU.subtract).then_inc(d_ready, 1)
                            for k in range(1, KD):
                                dve.wait_ge(lsq, L * KD + k + 1)
                                if k == 1:
                                    v_.tensor_tensor(acc[:, :], sq[:, 0, :], sq[:, 1, :], ALU.add).then_inc(lsum, 1)
                                else:
                                    dve.wait_ge(lsum, L * (KD - 1) + k - 1)
                                    v_.tensor_tensor(acc[:, :], acc[:, :], sq[:, k % 2, :], ALU.add).then_inc(lsum, 1)
                        if i == 3 and q == 0:
                            dve.wait_ge(lr_ready, L + 1)
                            for k in range(KD):
                                v_.tensor_tensor(cv[:, k, :], cv[:, k, :], rbc[:, :], ALU.mult).then_inc(n_ready, 1)
                        split(s4 + S_SSDO // 4 + i, q)
                        if q % 2:
                            m = 2 * i + q // 2
                            dve.wait_ge(slab_done, (s4 + i) * 4 + (S_SSDO + q + 1) + RING)
                            dve.wait_ge(gate_ready, L * 2 * KD + m + 1)
                            v_.scalar_tensor_tensor(out=mix[:, m, :], in0=mix[:, m, :], scalar=1.0, in1=bank[2 + m % 2][:, :],
                                                    op0=ALU.add, op1=ALU.mult).then_inc(mix_b, 1)
                for k in range(KD):
                    dve.wait_ge(chi_ready, L * KD + k + 1)
                    v_.tensor_tensor(hlo[:, k, :], cv[:, k, :], f32(hhi[:, k, :]), ALU.subtract).then_inc(c_split, 1)
                with dve.Fori(0, KD // 4) as i:
                    for q in range(4):
                        idx = L * KD + i * 4 + q
                        split(s4 + S_CONF // 4 + i, q)
                        dve.wait_ge(slab_done, (s4 + i) * 4 + (S_CONF + q + 1) + RING)
                        m = bass.ds(i * 4 + q, 1)
                        v_.scalar_tensor_tensor(out=mtmp[:, q % 2:q % 2 + 1, :], in0=ga[:, m, :], scalar=1.0,
                                                in1=bank[q % 2][:, :].unsqueeze(1), op0=ALU.add, op1=ALU.mult).then_inc(ya_mid, 1)
                        dve.wait_ge(ya_mid, idx + 3)
                        dve.wait_ge(mix_b, idx + 1)
                        v_.tensor_tensor(mix[:, m, :], mix[:, m, :], mtmp[:, q % 2:q % 2 + 1, :], ALU.add).then_inc(mix_ready, 1)
                        dve.wait_ge(mhi_ready, idx + 1)
                        v_.tensor_tensor(ulo[:, m, :], mix[:, m, :], f32(uhi[:, m, :]), ALU.subtract).then_inc(m_split, 1)
                update_x(s4 + S_WO // 4, 2, L * XL + X_WO, L * 3 + 2)
                ffn(L, 1, S_FFN2)
            add_square(3 * DEPTH, KD - 1)
            dve.wait_ge(r_ready, 3 * DEPTH + 1)
            for k in range(KD):
                v_.scalar_tensor_tensor(out=yfin[:, k, :], in0=xf[:, k, :], scalar=prm2[:, 0, P_FIN + k:P_FIN + k + 1],
                                        in1=rbc[:, :], op0=ALU.mult, op1=ALU.mult).then_inc(fin_ready, 1)

        @block.tensor
        def _(pe):
            t_ = nc.tensor

            def three(out, slot, k0, nk, hi, lo, start, stop, at=0):
                for k in range(nk):
                    w = slice((k0 + k) * P, (k0 + k + 1) * P)
                    for a, b in ((whi, hi), (whi, lo), (wlo, hi)):
                        ins = t_.matmul(out, a[:, slot, w], b[:, at + k, :], start=start and k == 0 and a is whi and b is hi,
                                        stop=stop and k == nk - 1 and a is wlo)
                return ins

            def slab(s, q, out, hi, lo, nk=8, start=True, stop=True):
                pe.wait_ge(lo_ready, s + 1 + RING)
                three(out, q, 0, nk, hi, lo, start, stop).then_inc(slab_done, 1)

            pe.wait_ge(const_fix, 7)
            pe.wait_ge(x_in, 32)
            for m in range(KD):
                if m >= 2:
                    pe.wait_ge(x_done, m - 1)
                for c in range(NC):
                    ins = t_.transpose(bank[m % 2][:, chunk(c)], x_tm[:, c, m * P:(m + 1) * P], ident[:, :])
                ins.then_inc(x_ps, 1)
            pe.wait_ge(consts_in, NCONST * 16)
            pe.wait_ge(v_out, 16)
            pe.wait_ge(y_out, 16)
            pe.wait_ge(c_out, 16)
            for l in range(DEPTH):
                col = 0
                for b, rows in enumerate(BROWS):
                    if b == len(BROWS) - 1:
                        ins.then_inc(prm_ps, 1)
                        col = 0
                    ins = t_.transpose(bank[2 + 2 * l + (b == len(BROWS) - 1)][:, col:col + rows],
                                       stage[0:rows, 5 * l + b, :], ident[0:rows, 0:rows])
                    col += rows
                ins.then_inc(prm_ps, 1)

            def stats(N):
                pe.wait_ge(sq_added, (N + 1) * (KD - 1) + 1)
                t_.matmul(bank[6][:, :], ones[:, :], acc[:, :], start=True, stop=True).then_inc(stat_mm, 1)

            def first_slab(s, q, out, hi, lo, ready, n, first=True, last=True, nk=KD):
                for k in range(nk):
                    pe.wait_ge(ready, n + k + 1)
                    if k == 0:
                        pe.wait_ge(lo_ready, s + 1 + RING)
                    ins = three(out, q, k, 1, hi, lo, first and k == 0, last and k == nk - 1, k)
                ins.then_inc(slab_done, 1)

            def ffn(L, f, base):
                N = L * 3 + 2 * f
                xb = L * XL + (KD if f == 0 else X_WO + 2 * KD)
                s = L * NSLAB + base

                def pair(s, PI, j):
                    pe.wait_ge(ab_free, PI + 1)
                    slab(s + 2 * j, 2 * j, bank[2 * j][:, :], uhi, ulo)
                    slab(s + 2 * j + 1, 2 * j + 1, bank[2 * j + 1][:, :], uhi, ulo)

                first_slab(s, 0, bank[0][:, :], uhi, ulo, u_ready, N * KD)
                stats(N)
                slab(s + 1, 1, bank[1][:, :], uhi, ulo)
                pair(s, L * (2 * FT) + (f * FT + 1), 1)
                for part, (p0, n) in enumerate(PARTS):
                    with pe.Fori(1 if part == 0 else 0, n // 2) as i:
                        for j in range(2):
                            pair(s + i * 4, L * (2 * FT) + (f * FT + p0 + j) + i * 2, j)
                    s = s + 2 * n
                    pe.wait_ge(x_done, xb + part * KD - 1)
                    first_slab(s, 0, bank[4][:, :], hhi, hlo, hlo_ready, L * (2 * FT) + (f * FT + p0), nk=n)
                    for q in range(1, 4):
                        pe.wait_ge(x_done, xb + part * KD + q - 1)
                        slab(s + q, q, bank[4 + q % 2][:, :], hhi, hlo, nk=n)
                    with pe.Fori(1, KD // 4) as i:
                        for q in range(4):
                            pe.wait_ge(x_done, xb + part * KD + i * 4 + q - 1)
                            slab(s + i * 4 + q, q, bank[4 + q % 2][:, :], hhi, hlo, nk=n)
                    s = s + KD

            def dt_steps(L, t):
                if t == 2:
                    pe.wait_ge(dt_dve, L * ND + 11)
                    pe.sem_inc(pe_passed, 1)
                    for j in range(2):
                        for c in range(NC):
                            ins = t_.transpose(bank[6][:, (j * NC + c) * 2 * NH:(j * NC + c + 1) * 2 * NH], dtf[:, j, chunk(c)], ident[0:2 * NH, 0:2 * NH])
                    ins.then_inc(dtr_ps, 1)
                if t == 3:
                    pe.wait_ge(dtr_ev, L * 2 + 2)
                    for c in range(NC):
                        ins = t_.matmul(bank[2 + c // 2][0:2 * NH, (c % 2) * 2 * P:(c % 2 + 1) * 2 * P], aT[:, c, :],
                                        ul[:, :, :].rearrange("p d i -> p (d i)"), start=True, stop=True)
                    ins.then_inc(rt_ps, 1)
                    cum = bank[4][:, 0:256].rearrange("p (c x) -> p c x", c=NC)
                    for d in range(2):
                        t_.matmul(cum[:, :, d * NH:(d + 1) * NH], ul[:, d, :], aT[:, :, d * NH:(d + 1) * NH], start=True, stop=True)
                    t_.matmul(bank[4][:, 256:512], ones[:, :], aT[:, :, :].rearrange("p c x -> p (c x)"), start=True, stop=True).then_inc(cum_ps, 1)

            def group(L, g, slabs, ssd, norm, gate=None):
                G = L * NG + g
                H, n = G - 1, G - 2
                s = L * NSLAB + g * 8 + S_GROUP

                def seg(c):
                    for d in range(2):
                        out = bank[2 + 4 * (c % 2) + d][:, :]
                        heads = out.rearrange("p (h i) -> p h i", h=HPG)
                        t_.matmul(heads, rtm[:, c, :], selg[:, 1, d, :].unsqueeze(2).broadcast_to([P, HPG, P]), start=True, stop=False,
                                  skip_group_check=True)
                        t_.matmul(heads, identr[:, :], never[:, d, :].unsqueeze(1).broadcast_to([P, HPG, P]), start=False, stop=False,
                                  skip_group_check=True)
                        for h in range(HPG):
                            ins = t_.matmul(out[:, chunk(h)], selg[:, 0, d, h:h + 1].broadcast_to([P, P]), rt[:, c, :],
                                            start=False, stop=h == HPG - 1, skip_group_check=True)
                    ins.then_inc(seg_ps, 1)

                def y_chunks(b):
                    for c in (2 * b, 2 * b + 1):
                        pe.wait_ge(m_ready, H * NC + c + 2)
                        for h in range(HPG):
                            f = (c % 2) * GF + h * HEAD
                            ins = t_.matmul(bank[4][:, f:f + HEAD], E[:, c, 0, chunk(h)],
                                            xT[:, c, h * HEAD:(h + 1) * HEAD], start=True, stop=True)
                    ins.then_inc(y_ps, 1)

                def y_transposed(b):
                    pe.wait_ge(y_ready, H * NB + b + 2)
                    pe.wait_ge(gated, H * NB + b + 1)
                    for c in range(2):
                        for j in range(2):
                            f = c * GF + j * P
                            ins = t_.transpose(bank[5][:, f:f + P], ytm[:, c, j * P:(j + 1) * P], ident[:, :])
                    ins.then_inc(yt_ps, 1)

                if gate is None:
                    free = [(z_ready, G * 2 + 1), (z_ready, G * 2 + 2), (tg_ready, G + 1), (v_ready, G + 1),
                            (pad_ready, G * 4 + 3), (pad_ready, G * 4 + 4), (pad_ready, G * 4 + 5), (pad_ready, G * 4 + 6)]
                else:
                    free = [(gate_ready, L * 2 * KD + gate + t - 1) for t in range(8)]
                    if gate == 0:
                        free[0:2] = [(z_ready, G * 2 + 1), (z_ready, G * 2 + 2)]
                for t in range(8):
                    if (slabs and (ssd or t)) or gate is not None:
                        pe.wait_ge(*free[t])
                        slab(s + t, t % RING, bank[t % 2][:, :], uhi, ulo)
                    if slabs and not ssd:
                        dt_steps(L, t)
                    if t == 0 and ssd:
                        pe.wait_ge(bc_ready, H * 4 + 4)
                        pe.wait_ge(e_ready, H * 2 * NC + 1)
                        for c in range(NC):
                            for j in range(2):
                                ins = t_.transpose(bank[2 + c // 2][:, (c % 2) * GF + j * P:(c % 2) * GF + (j + 1) * P],
                                                   bc[:, 2 + j, chunk(c)], ident[:, :])
                            if c % 2:
                                ins.then_inc(xt_ps, 1)
                        pe.wait_ge(y_ready, H * NB + 1)
                        for c in range(NC):
                            ins = t_.transpose(bank[4][:, chunk(c)], bc[:, 0, chunk(c)], ident[:, :])
                        ins.then_inc(bt_ps, 1)
                        pe.wait_ge(gated, H * NB + 1)
                        for c in range(NC):
                            ins = t_.matmul(bank[5][:, chunk(c)], bc[:, 0, chunk(c)], bc[:, 1, chunk(c)], start=True, stop=True)
                        ins.then_inc(sc_ps, 1)
                    if t == 1 and norm:
                        pe.wait_ge(gsq_sum, n + 1)
                        if ssd:
                            pe.wait_ge(bt_ready, H + 1)
                        t_.matmul(bank[4][:, :], ones[:, :], sq[:, 0, :], start=True, stop=True).then_inc(gst_ps, 1)
                    if t == 1 and ssd:
                        pe.wait_ge(xt_ready, H * 2 + 2)
                        pe.wait_ge(small_ready, H * 4 + 4)
                        pe.wait_ge(rt_ready, L * 5 + 5)
                        seg(0)
                        pe.wait_ge(yoff_ready, H * NB + 1)
                        seg(1)
                    if t == 2 and ssd:
                        for c in (2, 3):
                            pe.wait_ge(e_ready, H * 2 * NC + 2 * (c - 2) + 3)
                            seg(c)
                    if t == 3 and ssd:
                        pe.wait_ge(xw_ready, H + 2)
                        pe.wait_ge(bt_ready, H + 1)
                        pe.wait_ge(e_ready, H * 2 * NC + 2 * NC + 1)
                        for c in range(NC):
                            ins = t_.matmul(bank[6 + c // 2][:, (c % 2) * GF:(c % 2 + 1) * GF], bT[:, c, :], xw[:, c, :], start=True, stop=True)
                            if c % 2:
                                ins.then_inc(st_ps, 1)
                    if t == 4 and ssd:
                        pe.wait_ge(st_ready, H * 2 + 2)
                        for c in range(NC):
                            ins = t_.matmul(bank[6 + c // 2][:, (c % 2) * GF:(c % 2 + 1) * GF], bc[:, 1, chunk(c)],
                                            xw[:, c ^ 1, :], start=True, stop=True)
                            if c % 2:
                                ins.then_inc(yoff_ps, 1)
                        if norm:
                            pe.wait_ge(gln, n + 1)
                        y_chunks(0)
                    if t == 5 and ssd:
                        y_transposed(0)
                        y_chunks(1)
                    if t == 6 and ssd:
                        y_transposed(1)

            with pe.Fori(0, DEPTH) as L:
                ffn(L, 0, 0)
                stats(L * 3 + 1)
                pe.wait_ge(wd_lo_ready, L + 1)
                pe.wait_ge(z_ready, L * NG * 2 + 1)
                pe.wait_ge(lo_ready, L * NSLAB + (S_GROUP + 1 + RING))
                for k in range(KD):
                    pe.wait_ge(u_ready, L * 3 * KD + (KD + k + 1))
                    for a, b in ((wd_hi, uhi), (wd_hi, ulo), (wd_lo, uhi)):
                        ins = t_.matmul(bank[5][:, :], a[:, k, :], b[:, k, :], start=k == 0 and a is wd_hi and b is uhi,
                                        stop=k == KD - 1 and a is wd_lo)
                    if k == KD - 1:
                        ins.then_inc(dt_ps, 1)
                    ins = three(bank[0][:, :], 0, k, 1, uhi, ulo, k == 0, k == KD - 1, k)
                ins.then_inc(slab_done, 1)
                group(L, 0, True, False, False)
                group(L, 1, True, True, False)
                with pe.Fori(2, NG) as g:
                    group(L, g, True, True, True)
                group(L, NG, False, True, True, gate=0)
                group(L, NG + 1, False, False, True, gate=KD)
                s = L * NSLAB
                for i in range(KD // 2):
                    for q in range(4):
                        m = 2 * i + q // 2
                        if i == 0 and q < 2:
                            hi, lo = (phi, plo) if q else (hhi, hlo)
                            first_slab(s + (S_SSDO + q), q, bank[2][:, :], hi, lo, y_split, L * XT_ + (q * KD + 4), q == 0, q == 1)
                            continue
                        if q % 2 == 0 and m >= 2:
                            pe.wait_ge(mix_b, L * KD + m - 1)
                        hi, lo = (phi, plo) if q % 2 else (hhi, hlo)
                        slab(s + i * 4 + (S_SSDO + q), q, bank[2 + m % 2][:, :], hi, lo, start=q % 2 == 0, stop=q % 2 == 1)
                    if i == 1:
                        pe.wait_ge(cv_sum, (L + 1) * (KD - 1))
                        t_.matmul(bank[6][:, :], ones[:, :], acc[:, :], start=True, stop=True).then_inc(mu_ps, 1)
                    if i == 2:
                        pe.wait_ge(lsum, (L + 1) * (KD - 1))
                        t_.matmul(bank[7][:, :], ones[:, :], acc[:, :], start=True, stop=True).then_inc(lst_ps, 1)
                pe.wait_ge(gate_ready, L * 2 * KD + 2 * KD)
                first_slab(s + S_CONF, 0, bank[0][:, :], hhi, hlo, c_split, L * KD)
                for m in range(1, KD):
                    pe.wait_ge(ya_mid, L * KD + m + 1)
                    slab(s + (S_CONF + m), m % RING, bank[m % 2][:, :], hhi, hlo)
                first_slab(s + S_WO, 0, bank[2][:, :], uhi, ulo, m_split, L * KD)
                for m in range(1, KD):
                    pe.wait_ge(x_done, L * XL + (X_WO + KD - 1) + m)
                    slab(s + (S_WO + m), m % RING, bank[2 + m % 2][:, :], uhi, ulo)
                ffn(L, 1, S_FFN2)
            stats(3 * DEPTH)
            for half in range(2):
                pe.wait_ge(fin_ready, (half + 1) * KD // 2)
                for c in range(NC):
                    if half:
                        pe.wait_ge(out_ready, c + 1)
                    for k in range(4):
                        ins = t_.transpose(bank[c][:, chunk(k)], yfin[:, half * 4 + k, chunk(c)], ident[:, :])
                    ins.then_inc(out_ps, 1)


_INS = ["x_prompt", "x_sample", "ffn1_norm", "ffn1_w_up", "ffn1_w_down", "mix_norm", "w_in", "gate_bias",
        "conf_dw_w", "conf_dw_b", "conf_ln_g", "conf_ln_b", "conf_w_out", "ssd_conv_w", "ssd_conv_b",
        "ssd_dt_bias", "ssd_A_log", "ssd_D", "ssd_norm", "ssd_w_out", "w_o", "ffn2_norm", "ffn2_w_up",
        "ffn2_w_down", "final_norm"]


def kernel(**inputs):
    import numpy as _np
    import concourse.bacc as _bacc
    from concourse import mybir as _mybir
    from concourse.bass_utils import run_bass_kernel_spmd as _run

    nc = _bacc.Bacc("TRN2", target_bir_lowering=False, num_devices=1)
    arrays, io = {}, {}
    for name in _INS:
        a = _np.ascontiguousarray(inputs[name])
        arrays[f"in_{name}"] = a
        io[name] = nc.dram_tensor(f"in_{name}", a.shape, _mybir.dt.from_np(a.dtype), kind="ExternalInput").ap()
    for i, name in enumerate(("x_prompt", "x_sample")):
        a = arrays[f"in_{name}"]
        io[f"out_{i}"] = nc.dram_tensor(f"out_{i}", a.shape, _mybir.dt.from_np(a.dtype), kind="ExternalOutput").ap()
    trunk(nc, io)
    r = _run(nc, [arrays], core_ids=[0])
    return tuple(r.results[0][f"out_{i}"] for i in range(2))
```
